# Optimizing a Trainium2 kernel written in Bass

```python
import math, functools
import jax, jax.numpy as jnp
from jax import lax
import numpy as np

D_MODEL = 1024
BATCH = 1
SEQ = 1024
DEPTH = 1
DEC_BATCH = 8
DEC_SEQ = 8
PAST_LEN = 1024
PAGE_SIZE = 128

N_HEADS = 8
HEAD_DIM = 64
V_DIM = 2 * HEAD_DIM
QK_WIDTH = N_HEADS * 2 * HEAD_DIM
ATTN_WIDTH = N_HEADS * V_DIM
POOL_WINDOWS = (2, 4, 8, 16)
N_POOL_GROUPS = len(POOL_WINDOWS)
POOL_WIDTH = 1024
POOL_GROUP = POOL_WIDTH // N_POOL_GROUPS
POOL_BUF = max(POOL_WINDOWS) - 1
D_FF = 2816
CONV_W = 3
FFN_BUF = CONV_W - 1
Q_BLOCK = 128
EPS = 1e-6
NEG = -1e30
IN_WIDTH = 2 * QK_WIDTH + ATTN_WIDTH + POOL_WIDTH + 2 * D_MODEL
SPLITS = (QK_WIDTH, 2 * QK_WIDTH, 2 * QK_WIDTH + ATTN_WIDTH,
          2 * QK_WIDTH + ATTN_WIDTH + POOL_WIDTH,
          2 * QK_WIDTH + ATTN_WIDTH + POOL_WIDTH + D_MODEL)

kernel_name = "diffattn_pool_gated_hybrid_step"

def lambda_init_for(layer):
    return 0.8 - 0.6 * math.exp(-0.3 * layer)

def rms_norm(x, g):
    xf = x.astype(jnp.float32)
    y = xf * lax.rsqrt(jnp.mean(xf * xf, axis=-1, keepdims=True) + EPS)
    return (y * g.astype(jnp.float32)).astype(x.dtype)

def diff_probs(scores, lam):
    p = jax.nn.softmax(scores, axis=-1)
    return p[:, :, 0] - lam * p[:, :, 1]

def prompt_attention(q, k, v, lam):
    b, t = q.shape[:2]
    nb = t // Q_BLOCK
    qb = q.reshape(b, nb, Q_BLOCK, N_HEADS, 2, HEAD_DIM).transpose(1, 0, 2, 3, 4, 5)
    kpos = jnp.arange(t)
    scale = HEAD_DIM ** -0.5

    def one_block(args):
        i, qi = args
        qpos = i * Q_BLOCK + jnp.arange(Q_BLOCK)
        s = jnp.einsum('bqhcd,bkhcd->bhcqk', qi, k, preferred_element_type=jnp.float32) * scale
        s = jnp.where(kpos[None, :] <= qpos[:, None], s, NEG)
        p = diff_probs(s, lam).astype(v.dtype)
        return jnp.einsum('bhqk,bkhe->bqhe', p, v)

    o = lax.map(one_block, (jnp.arange(nb), qb))
    return o.transpose(1, 0, 2, 3, 4).reshape(b, t, N_HEADS, V_DIM)

def sample_attention(q, k_new, v_new, lam, k_cache, v_cache, page_table, layer):
    b, t = q.shape[:2]
    k_past = k_cache[layer, page_table].reshape(b, -1, N_HEADS, 2, HEAD_DIM)
    v_past = v_cache[layer, page_table].reshape(b, -1, N_HEADS, V_DIM)
    n_past = k_past.shape[1]
    scale = HEAD_DIM ** -0.5
    s_past = jnp.einsum('bqhcd,bkhcd->bhcqk', q, k_past, preferred_element_type=jnp.float32)
    s_new = jnp.einsum('bqhcd,bkhcd->bhcqk', q, k_new, preferred_element_type=jnp.float32)
    s_new = jnp.where(jnp.tril(jnp.ones((t, t), dtype=bool)), s_new, NEG)
    s = jnp.concatenate([s_past, s_new], axis=-1) * scale
    p = diff_probs(s, lam).astype(v_new.dtype)
    return (jnp.einsum('bhqk,bkhe->bqhe', p[..., :n_past], v_past)
            + jnp.einsum('bhqk,bkhe->bqhe', p[..., n_past:], v_new))

def pool_mixer(u, prefix, p0, w_pool, pool_scale):
    b, t, _ = u.shape
    ext_raw = jnp.concatenate([prefix, u], axis=1)
    ext = ext_raw.astype(jnp.float32)
    cs = jnp.concatenate([jnp.zeros((b, 1, POOL_WIDTH), jnp.float32), jnp.cumsum(ext, axis=1)], axis=1)
    pos = p0 + jnp.arange(t)
    outs = []
    for g, w in enumerate(POOL_WINDOWS):
        c0, c1 = g * POOL_GROUP, (g + 1) * POOL_GROUP
        hi = cs[:, POOL_BUF + 1:POOL_BUF + 1 + t, c0:c1]
        lo = cs[:, POOL_BUF + 1 - w:POOL_BUF + 1 - w + t, c0:c1]
        cnt = jnp.minimum(w, pos + 1).astype(jnp.float32)[None, :, None]
        d = ((hi - lo) / cnt - ext[:, POOL_BUF:, c0:c1]).astype(u.dtype)
        outs.append(jnp.einsum('btc,cd->btd', d, w_pool[g]) * pool_scale[g])
    return jnp.concatenate(outs, axis=-1), ext_raw[:, -POOL_BUF:]

def conv_ffn(h, prefix, w_up, conv_w, conv_b, w_down):
    t = h.shape[1]
    up = h @ w_up
    ext = jnp.concatenate([prefix, up], axis=1)
    c = conv_b + sum(ext[:, j:j + t] * conv_w[j] for j in range(CONV_W))
    gate, val = jnp.split(c, 2, axis=-1)
    return (jax.nn.silu(gate) * val) @ w_down, ext[:, -FFN_BUF:]

def decoder_layer(x, attention_fn, pool_prefix, ffn_prefix, p0, lam_init, lp):
    (norm_mix, w_in, q_norm, k_norm, lq1, lk1, lq2, lk2, head_norm, w_pool, pool_scale,
     w_attn_branch, w_pool_branch, w_out, norm_ffn, w_up, conv_w, conv_b, w_down) = lp
    b, t, _ = x.shape
    h = rms_norm(x, norm_mix)
    q, k, v, u, ga, gp = jnp.split(h @ w_in, SPLITS, axis=-1)
    q = rms_norm(q.reshape(b, t, N_HEADS, 2, HEAD_DIM), q_norm)
    k = rms_norm(k.reshape(b, t, N_HEADS, 2, HEAD_DIM), k_norm)
    v = v.reshape(b, t, N_HEADS, V_DIM)
    f32 = jnp.float32
    lam = (jnp.exp(jnp.sum(lq1.astype(f32) * lk1.astype(f32)))
           - jnp.exp(jnp.sum(lq2.astype(f32) * lk2.astype(f32))) + lam_init)
    o = attention_fn(q, k, v, lam)
    o = (rms_norm(o, head_norm) * (1.0 - lam_init)).reshape(b, t, ATTN_WIDTH)
    pool_o, pool_state = pool_mixer(u, pool_prefix, p0, w_pool, pool_scale)
    merged = jax.nn.sigmoid(ga) * (o @ w_attn_branch) + jax.nn.sigmoid(gp) * (pool_o @ w_pool_branch)
    x1 = x + merged @ w_out
    f, ffn_state = conv_ffn(rms_norm(x1, norm_ffn), ffn_prefix, w_up, conv_w, conv_b, w_down)
    return x1 + f, k.reshape(b, t, N_HEADS, 2 * HEAD_DIM), v, pool_state, ffn_state

def setup_inputs(seed: int = 0) -> dict:
    key = jax.random.key(seed)
    ks = jax.random.split(key, 32)
    n_pages = PAST_LEN // PAGE_SIZE
    n_used = DEC_BATCH * n_pages
    n_phys = n_used + max(1, n_used // 4)
    nrm = jax.random.normal
    f = jnp.float32
    page_table = jax.random.permutation(ks[0], n_phys)[:n_used].reshape(DEC_BATCH, n_pages).astype(jnp.int32)
    return {
        'x_prompt': nrm(ks[1], (BATCH, SEQ, D_MODEL), f),
        'x_sample': nrm(ks[2], (DEC_BATCH, DEC_SEQ, D_MODEL), f),
        'cache_k': nrm(ks[3], (DEPTH, n_phys, PAGE_SIZE, N_HEADS, 2 * HEAD_DIM), f),
        'cache_v': nrm(ks[4], (DEPTH, n_phys, PAGE_SIZE, N_HEADS, V_DIM), f),
        'state_pool': nrm(ks[5], (DEPTH, DEC_BATCH, POOL_BUF, POOL_WIDTH), f),
        'state_ffn_conv': nrm(ks[6], (DEPTH, DEC_BATCH, FFN_BUF, 2 * D_FF), f),
        'page_table': page_table,
        'norm_mix': 1.0 + 0.02 * nrm(ks[7], (DEPTH, D_MODEL), f),
        'w_in': nrm(ks[8], (DEPTH, D_MODEL, IN_WIDTH), f) * D_MODEL ** -0.5,
        'q_norm': 1.0 + 0.02 * nrm(ks[9], (DEPTH, 2, HEAD_DIM), f),
        'k_norm': 1.0 + 0.02 * nrm(ks[10], (DEPTH, 2, HEAD_DIM), f),
        'lambda_q1': 0.1 * nrm(ks[11], (DEPTH, HEAD_DIM), f),
        'lambda_k1': 0.1 * nrm(ks[12], (DEPTH, HEAD_DIM), f),
        'lambda_q2': 0.1 * nrm(ks[13], (DEPTH, HEAD_DIM), f),
        'lambda_k2': 0.1 * nrm(ks[14], (DEPTH, HEAD_DIM), f),
        'head_norm': 1.0 + 0.02 * nrm(ks[15], (DEPTH, N_HEADS, V_DIM), f),
        'w_pool': nrm(ks[16], (DEPTH, N_POOL_GROUPS, POOL_GROUP, POOL_GROUP), f) * POOL_GROUP ** -0.5,
        'pool_scale': 1.0 + 0.1 * nrm(ks[17], (DEPTH, N_POOL_GROUPS, POOL_GROUP), f),
        'w_attn_branch': nrm(ks[18], (DEPTH, ATTN_WIDTH, D_MODEL), f) * ATTN_WIDTH ** -0.5,
        'w_pool_branch': nrm(ks[19], (DEPTH, POOL_WIDTH, D_MODEL), f) * POOL_WIDTH ** -0.5,
        'w_out': nrm(ks[20], (DEPTH, D_MODEL, D_MODEL), f) * D_MODEL ** -0.5,
        'norm_ffn': 1.0 + 0.02 * nrm(ks[21], (DEPTH, D_MODEL), f),
        'w_up': nrm(ks[22], (DEPTH, D_MODEL, 2 * D_FF), f) * D_MODEL ** -0.5,
        'conv_w': nrm(ks[23], (DEPTH, CONV_W, 2 * D_FF), f) * CONV_W ** -0.5,
        'conv_b': 0.02 * nrm(ks[24], (DEPTH, 2 * D_FF), f),
        'w_down': nrm(ks[25], (DEPTH, D_FF, D_MODEL), f) * D_FF ** -0.5,
    }

def reference(x_prompt, x_sample, cache_k, cache_v, state_pool, state_ffn_conv, page_table,
              norm_mix, w_in, q_norm, k_norm, lambda_q1, lambda_k1, lambda_q2, lambda_k2,
              head_norm, w_pool, pool_scale, w_attn_branch, w_pool_branch, w_out,
              norm_ffn, w_up, conv_w, conv_b, w_down):
    yp, ys = x_prompt, x_sample
    kp_l, vp_l, pp_l, fp_l, ks_l, vs_l, ps_l, fs_l = [], [], [], [], [], [], [], []
    for l in range(DEPTH):
        lam_init = lambda_init_for(l)
        lp = (norm_mix[l], w_in[l], q_norm[l], k_norm[l], lambda_q1[l], lambda_k1[l],
              lambda_q2[l], lambda_k2[l], head_norm[l], w_pool[l], pool_scale[l],
              w_attn_branch[l], w_pool_branch[l], w_out[l], norm_ffn[l], w_up[l],
              conv_w[l], conv_b[l], w_down[l])
        pool_prefix = jnp.zeros((yp.shape[0], POOL_BUF, POOL_WIDTH), yp.dtype)
        ffn_prefix = jnp.zeros((yp.shape[0], FFN_BUF, 2 * D_FF), yp.dtype)
        yp, kp, vp, pp, fp = decoder_layer(yp, prompt_attention, pool_prefix, ffn_prefix, 0, lam_init, lp)
        attn_s = functools.partial(sample_attention, k_cache=cache_k, v_cache=cache_v,
                                   page_table=page_table, layer=l)
        ys, k_s, v_s, p_s, f_s = decoder_layer(ys, attn_s, state_pool[l], state_ffn_conv[l],
                                              PAST_LEN, lam_init, lp)
        kp_l.append(kp); vp_l.append(vp); pp_l.append(pp); fp_l.append(fp)
        ks_l.append(k_s); vs_l.append(v_s); ps_l.append(p_s); fs_l.append(f_s)
    return (yp, ys,
            jnp.stack(kp_l), jnp.stack(vp_l), jnp.stack(pp_l), jnp.stack(fp_l),
            jnp.stack(ks_l), jnp.stack(vs_l), jnp.stack(ps_l), jnp.stack(fs_l))


_drawn_inputs = setup_inputs


def setup_inputs(seed=0):
    import zlib

    import numpy as np

    out = dict(_drawn_inputs(seed))
    spreads = {}
    factors = {'norm_mix': 2.831,
     'q_norm': 5.972,
     'lambda_k2': 3.767,
     'head_norm': 7.149,
     'norm_ffn': 2.752,
     'conv_b': 4.334}
    for name, (base, spread) in spreads.items():
        noise = np.random.default_rng([zlib.crc32(name.encode()), seed]).standard_normal(out[name].shape)
        drawn = base * np.exp(spread * noise) if base else spread * noise
        out[name] = __import__('jax').numpy.asarray(drawn.astype(out[name].dtype))
    for name, factor in factors.items():
        out[name] = (out[name] * factor).astype(out[name].dtype)
    return out
```

```python
from contextlib import ExitStack

import concourse.bass as bass
from concourse import mybir

F32 = mybir.dt.float32
F32R = mybir.dt.float32r
I32 = mybir.dt.int32
ALU = mybir.AluOpType
ACT = mybir.ActivationFunctionType
AX = mybir.AxisListType

P = 128
EPS = 1e-6
NEG = -1e30
LAMBDA_INIT = 0.2


def build_step(
    nc, x_prompt, x_sample, cache_k, cache_v, state_pool, state_ffn_conv, page_table,
    norm_mix, w_in, q_norm, k_norm, lambda_q1, lambda_k1, lambda_q2, lambda_k2, head_norm,
    w_pool, pool_scale, w_attn_branch, w_pool_branch, w_out, norm_ffn, w_up, conv_w, conv_b, w_down,
    y_prompt, y_sample, k_prompt, v_prompt, pool_prompt, ffn_prompt,
    k_sample, v_sample, pool_sample, ffn_sample,
):
    D = x_prompt.shape[2]
    KT = D // P
    SEQ = x_prompt.shape[1]
    NB, NS = x_sample.shape[0], x_sample.shape[1]
    NSAMP = NB * NS
    TOK = SEQ + NSAMP
    QT = SEQ // P
    TT = QT + 1
    NH, VD = cache_k.shape[3], cache_k.shape[4]
    HD = VD // 2
    PAGE = cache_k.shape[2]
    NPG = page_table.shape[1]
    NPHYS = cache_k.shape[1]
    PASTK = NPG * PAGE
    BUF = state_pool.shape[2]
    NG, GW = w_pool.shape[1], w_pool.shape[2]
    FF2 = w_up.shape[2]
    FT = FF2 // 2 // P
    SCALE = HD ** -0.5
    assert (D, SEQ, NH, VD, PAGE, NSAMP, QT) == (NH * VD, QT * P, 8, P, P, 64, 8)
    COL_U, COL_GA, COL_GP = 3 * D, 4 * D, 5 * D
    CW = 3 * P
    CHUNKS = [(0, CW), (CW, CW), (2 * CW, TOK - 2 * CW)]

    def rows(t):
        return P if t < QT else NSAMP

    base = -(-nc.sbuf_base // 64) * 64
    C0 = base
    R1 = C0 + 8192
    R1_BYTES = 2 * KT * TOK * 4
    X0 = R1 + R1_BYTES
    X_END = nc.sbuf_usable_end // 32 * 32

    def at(name, shape, dt, offset):
        n = 4
        for s in shape[1:]:
            n *= s
        assert offset >= base and offset + n <= X_END, (name, offset + n - X_END)
        return nc.alloc_sbuf_tensor_at(name, shape, dt, offset=offset)

    def fit(*shape):
        n = 4
        for s in shape:
            n *= s
        return -(-n // 32) * 32

    class Region:

        def __init__(self, start, end):
            self.at, self.end = start, end

        def __call__(self, name, shape, dt=F32):
            n = 4
            for s in shape[1:]:
                n *= s
            t = at(name, shape, dt, self.at)
            self.at += -(-n // 32) * 32
            assert self.at <= self.end, (name, self.at - self.end)
            return t

    const = Region(C0, R1)
    ident = const("ident", [P, P])
    causal = const("causal", [P, P])
    gain_qk = const("gain_qk", [P, 2 * VD])
    late_at = const.at
    qT_s = const("qT_s", [P, NH, NSAMP])
    kT_s = const("kT_s", [P, NH + 1, NSAMP])
    pick = const("pick", [P, P])
    new_mask = const("new_mask", [P, NS])
    neghalf = const("neghalf", [P, 12])
    eps_t = const("eps_t", [P, 12])
    inv_n = {n: const(f"inv_n{n}", [P, 12]) for n in (HD, VD, D)}
    ss = const("ss", [P, 12])
    rs = const("rs", [P, 12])
    row_max = const("row_max", [P, 2, 2])
    negm = const("negm", [P, 2, 2])
    den = const("den", [P, 2, 2])
    rden = const("rden", [P, 2, 2])
    neglam = const("neglam", [P, 1])
    lam_s = const("lam_s", [P, 4])
    coef = const("coef", [P, 1])
    sst = const("sst", [P, 4, 8])
    rst = const("rst", [P, 4, 8])
    inv_cnt = const("inv_cnt", [P, 16])
    gain_fm = const("gain_fm", [P, 16])

    act_hi = at("act_hi", [P, KT, TOK], F32R, R1)
    act_lo = at("act_lo", [P, KT, TOK], F32R, R1 + R1_BYTES // 2)

    r = Region(X0, X_END)
    w_raw = r("w_raw", [P, KT, 3, VD])
    w_hi = [r(f"w_hi{i}", [P, KT, 3, VD], F32R) for i in range(2)]
    w_lo = [r(f"w_lo{i}", [P, KT, 3, VD], F32R) for i in range(2)]
    raw_at = [r.at, r.at + fit(TT, 3 * VD)]
    raw = [r(f"raw{i}", [P, TT, 3 * VD]) for i in range(2)]
    qT = [r(f"qT{i}", [P, TOK]) for i in range(2)]
    kT = [r(f"kT{i}", [P, TOK]) for i in range(2)]
    e_at = r.at
    E = [r(f"E{i}", [P, 2, SEQ]) for i in range(2)]
    pt_at = r.at
    PTs = [r(f"PTs{i}", [P, 4 * P]) for i in range(2)]
    osb_at = r.at
    osb = r("osb", [P, QT, VD])
    sq = r("sq", [P, 3, 2 * VD])
    pgt_at = X_END - fit(NB * NPG)
    assert r.at <= pgt_at
    pgt = at("pgt", [1, NB * NPG], I32, pgt_at)
    rowi = at("rowi", [P, 3 * NS], I32, osb_at)
    xt = [at(f"xt{i}", [P, D], F32, e_at + i * D * 4) for i in range(3)]
    junk = at("junk", [P, D], F32, e_at + 3 * D * 4)
    gain_x = at("gain_x", [P, D], F32, pt_at)

    o_dram = nc.dram_tensor("o_scratch", [TOK, D], F32, kind="Internal").ap()

    ctx = ExitStack()
    with ctx:
        PS = ctx.enter_context(nc.psum_tensor("PS", [P, 8, 512], F32))
        scores_ps = PS[:, 0:4, :].rearrange("p (c b) n -> p c (b n)", c=2)
        PJ, B_PT, B_O = 4, 6, 7

        def sem(name):
            return ctx.enter_context(nc.semaphore(name))

        x_ld = [sem(f"x_ld{i}") for i in range(3)]
        gain_x_ld = sem("gain_x_ld")
        gain_ld = sem("gain_ld")
        lam_ld = sem("lam_ld")
        consts = sem("consts")
        sst_set = sem("sst_set")
        consts_step = sem("consts_step")
        lam_step = sem("lam_step")
        sumsq_x = sem("sumsq_x")
        rstd_x = sem("rstd_x")
        xn_x = sem("xn_x")
        tr_x = sem("tr_x")
        hi_x = sem("hi_x")
        lo_x = sem("lo_x")
        pool_step = sem("pool_step")
        dve_step = sem("dve_step")
        w0_ld = [sem(f"w0_ld{i}") for i in range(3)]
        w_ld = sem("w_ld")
        w_head = sem("w_head")
        w_tail = sem("w_tail")
        pj_full = sem("pj_full")
        pj_free = sem("pj_free")
        sumsq_qk = sem("sumsq_qk")
        rstd_qk = sem("rstd_qk")
        scaled_qk = sem("scaled_qk")
        gained_qk = sem("gained_qk")
        b7_full = sem("b7_full")
        b7_free = sem("b7_free")
        s_full = sem("s_full")
        negm_ready = sem("negm_ready")
        exp_done = sem("exp_done")
        p_ready = sem("p_ready")
        pt_full = sem("pt_full")
        pt_free = sem("pt_free")
        kv_st = [sem(f"kv_st{i}") for i in range(2)]
        o_st = sem("o_st")

        class Step:

            def __init__(self, eng, s):
                self.eng, self.s, self.n = eng, s, 0

            def __call__(self, ins):
                self.n = self.n + 1
                ins.then_inc(self.s, 1)
                self.eng.wait_ge(self.s, self.n)

        def bank_uses(proj):
            order, n = {}, 0
            for s in range(TT):
                if s == 2 or (proj and s in (5, 8)):
                    order["q", s], order["k", s] = n, n + 1
                    n += 2
                if s >= 1:
                    order["o", s] = n
                    n += 1
            return order, n

        USES, USES_PER = bank_uses(True)
        LAST_USES, LAST_USES_PER = bank_uses(False)
        FIRST_USES = 4
        PT_AT = [0, 1, 2, 3, 4, 6, 8, 10, 12]

        def b_use(h, proj, key):
            return FIRST_USES + h * USES_PER + (USES if proj else LAST_USES)[key]

        def pe_norm_transposes(e, t):
            e.wait_ge(xn_x, t + 1)
            for half in range(2):
                bank = 2 * (t % 2) + half
                if t >= 2:
                    e.wait_ge(lo_x, 2 * (t - 2) + half + 1)
                for j in range(4):
                    kt = 4 * half + j
                    ins = e.transpose(PS[:, bank, j * P:j * P + rows(t)],
                                      xt[t % 3][0:rows(t), kt * P:(kt + 1) * P],
                                      ident[0:rows(t), 0:rows(t)])
                ins.then_inc(tr_x, 1)

        def pe_project(e, n, slot, s, between, first=False):
            if s == 0 and not first:
                e.wait_ge(w_tail, n * 3 + 3)
            e.wait_ge(pj_free, n * TT + s + 1)
            bank = PJ + (slot + s) % 2
            for kt in range(KT):
                if kt in between:
                    between[kt]()
                if first and kt in (0, 3, 6):
                    e.wait_ge(w_tail, kt // 3 + 1)
                a_hi = act_hi[:, kt, s * P:s * P + rows(s)]
                a_lo = act_lo[:, kt, s * P:s * P + rows(s)]
                h3 = w_hi[slot][:, kt, :, :].rearrange("p a b -> p (a b)")
                l3 = w_lo[slot][:, kt, :, :].rearrange("p a b -> p (a b)")
                out = PS[0:rows(s), bank, 0:3 * VD]
                e.matmul(out, a_hi, h3, start=kt == 0, stop=False)
                e.matmul(out, a_hi, l3, start=False, stop=False)
                ins = e.matmul(out, a_lo, h3, start=False, stop=kt == KT - 1)
            ins.then_inc(pj_full, 1)

        def pe_qk_transposes(e, n, slot, g, use, parts=(0, 1)):
            for part in parts:
                if part == 0:
                    e.wait_ge(gained_qk, n * 3 + g + 1)
                e.wait_ge(b7_free, use + part)
                for j in range(3):
                    t = 3 * g + j
                    ins = e.transpose(PS[:, B_O, j * P:j * P + rows(t)],
                                      raw[slot][0:rows(t), t, part * VD:(part + 1) * VD],
                                      ident[0:rows(t), 0:rows(t)])
                ins.then_inc(b7_full, 1)

        def qk_group(h, slot, proj, s):
            if s == 2:
                return h, slot, 2, b_use(h, proj, ("q", 2))
            if proj and s in (5, 8):
                return h + 1, 1 - slot, s // 3 - 1, b_use(h, proj, ("q", s))
            return None

        def pe_scores(e, h, slot, s):
            if s == 0:
                e.wait_ge(b7_free, FIRST_USES + h * USES_PER)
            e.wait_ge(exp_done, h * QT + s + 1)
            n = (s + 1) * P
            for c in range(2):
                for b in range(0, n, 512):
                    w = min(512, n - b)
                    ins = e.matmul(PS[:, 2 * c + b // 512, 0:w],
                                   qT[slot][c * HD:(c + 1) * HD, s * P:(s + 1) * P],
                                   kT[slot][c * HD:(c + 1) * HD, b:b + w], start=True, stop=True)
            ins.then_inc(s_full, 1)

        def pe_probs_transpose(e, h, s, g):
            if g == 0:
                e.wait_ge(p_ready, h * QT + s + 1)
            use = h * PT_AT[QT] + PT_AT[s] + g
            e.wait_ge(pt_free, use + 1)
            for j in range(min(4, s + 1 - 4 * g)):
                kt = 4 * g + j
                ins = e.transpose(PS[:, B_PT, j * P:(j + 1) * P],
                                  E[s % 2][:, 0, kt * P:(kt + 1) * P], ident[:, :])
            ins.then_inc(pt_full, 1)

        def pe_values(e, h, slot, s, use_o):
            e.wait_ge(b7_free, use_o)
            for kt in range(s + 1):
                g = kt // 4
                use = h * PT_AT[QT] + PT_AT[s] + g
                if kt % 4 == 0:
                    e.wait_ge(pt_free, use + 2)
                ins = e.matmul(PS[:, B_O, 0:VD], PTs[(PT_AT[s] + g) % 2][:, (kt % 4) * P:(kt % 4 + 1) * P],
                               raw[slot][:, kt, 2 * VD:3 * VD], start=kt == 0, stop=kt == s)
            ins.then_inc(b7_full, 1)

        def pe_head(e, h, slot, proj):
            for s in range(TT):
                if s < QT:
                    pe_scores(e, h, slot, s)

                def first_group():
                    if s >= 1:
                        pe_probs_transpose(e, h, s - 1, 0)

                def second_group():
                    if s >= 5:
                        pe_probs_transpose(e, h, s - 1, 1)

                group = qk_group(h, slot, proj, s)

                def q_part():
                    if group:
                        pe_qk_transposes(e, *group, parts=(0,))

                def k_part():
                    if group:
                        pe_qk_transposes(e, *group, parts=(1,))

                if not proj:
                    first_group()
                    second_group()
                    q_part()
                    k_part()
                elif s == QT:
                    q_part()
                    pe_project(e, h + 1, 1 - slot, s, {5: k_part})
                    first_group()
                    second_group()
                elif s < 5:
                    q_part()
                    pe_project(e, h + 1, 1 - slot, s, {2: first_group, 5: k_part})
                else:
                    first_group()
                    q_part()
                    pe_project(e, h + 1, 1 - slot, s, {2: second_group, 5: k_part})
                if s >= 1:
                    pe_values(e, h, slot, s - 1, b_use(h, proj, ("o", s)))

        def pe_phase1(e):
            e.wait_ge(consts, 1)
            pe_norm_transposes(e, 0)
            for s in range(TT):
                if s + 1 < TT:
                    pe_norm_transposes(e, s + 1)
                e.wait_ge(lo_x, 2 * s + 2)
                pe_project(e, 0, 0, s, {}, first=s == 0)
                if s in (5, 8):
                    pe_qk_transposes(e, 0, 0, s // 3 - 1, 2 * (s // 3 - 1))
            with e.Fori(0, NH // 2 - 1) as i:
                for slot in range(2):
                    pe_head(e, i * 2 + slot, slot, True)
            pe_head(e, NH - 2, 0, True)
            pe_head(e, NH - 1, 1, False)

        SPLITS = [(0, 3), (3, 6), (6, KT)]

        def act_split_w(e, m, slot, piece):
            a, b = SPLITS[piece]
            if isinstance(m, int) and m == 0:
                e.wait_ge(w0_ld[piece], 48)
            elif piece == 0:
                e.wait_ge(w_ld, m * 48)
            e.activation(w_hi[slot][:, a:b, :, :], w_raw[:, a:b, :, :], ACT.Copy).then_inc(w_head, 1)

        def act_evac_projection(e, n, slot, s, stored):
            if s == 0:
                e.wait_ge(kv_st[slot], stored * 64 + 1)
            e.wait_ge(pj_full, n * TT + s + 1)
            e.activation(raw[slot][0:rows(s), s, :], PS[0:rows(s), PJ + (slot + s) % 2, 0:3 * VD],
                         ACT.Copy).then_inc(pj_free, 1)

        def act_evac_qk(e, n, slot, g, use, parts=(0, 1)):
            for part in parts:
                dst, dst_s = ((qT, qT_s), (kT, kT_s))[part]
                e.wait_ge(b7_full, use + part + 1)
                w = 3 * P if g < 2 else 2 * P + NSAMP
                if g < 2:
                    e.activation(dst[slot][:, 3 * g * P:3 * g * P + w], PS[:, B_O, 0:w],
                                 ACT.Copy).then_inc(b7_free, 1)
                else:
                    e.activation(dst_s[:, bass.ds(n, 1), :], PS[:, B_O, 2 * P:w].unsqueeze(1), ACT.Copy)
                    e.activation(dst[slot][:, 3 * g * P:3 * g * P + w], PS[:, B_O, 0:w],
                                 ACT.Copy).then_inc(b7_free, 1)

        def act_evac_probs(e, h, s, g):
            use = h * PT_AT[QT] + PT_AT[s] + g
            e.wait_ge(pt_full, use + 1)
            w = min(4, s + 1 - 4 * g) * P
            e.activation(PTs[(PT_AT[s] + g) % 2][:, 0:w], PS[:, B_PT, 0:w], ACT.Copy).then_inc(pt_free, 1)

        def act_exp(e, h, s):
            e.wait_ge(negm_ready, h * QT + s + 1)
            n = (s + 1) * P
            for c in range(2):
                ins = e.activation(E[s % 2][:, c, 0:n], scores_ps[:, c, 0:n], ACT.Exp,
                                   bias=negm[:, s % 2, c:c + 1], scale=SCALE,
                                   accum_out=den[:, s % 2, c:c + 1])
            ins.then_inc(exp_done, 1)

        def act_head(e, h, slot, proj, split, stored):
            for s in range(TT):
                if split and s in (0, 3, 6):
                    if s == 0:
                        e.wait_ge(pj_full, h * TT + TT)
                    act_split_w(e, h + 2, slot, s // 3)
                group = qk_group(h, slot, proj, s)
                if proj and s == QT:
                    act_evac_qk(e, *group)
                    act_evac_projection(e, h + 1, 1 - slot, s, stored)
                if s >= 1:
                    act_evac_probs(e, h, s - 1, 0)
                if group and proj and s < QT:
                    act_evac_qk(e, *group, parts=(0,))
                if s >= 5:
                    act_evac_probs(e, h, s - 1, 1)
                if s < QT:
                    act_exp(e, h, s)
                if group and proj and s < QT:
                    act_evac_qk(e, *group, parts=(1,))
                elif group and not proj:
                    act_evac_qk(e, *group)
                if proj and s < QT:
                    act_evac_projection(e, h + 1, 1 - slot, s, stored)
                if s >= 1:
                    use = b_use(h, proj, ("o", s))
                    if s == 1:
                        e.wait_ge(o_st, h * 16 + 1)
                    e.wait_ge(b7_full, use + 1)
                    e.activation(osb[:, s - 1, :], PS[:, B_O, 0:VD], ACT.Copy).then_inc(b7_free, 1)
            e.wait_ge(b7_free, use + 1)
            e.dma_start(o_dram[0:SEQ, bass.ds(h * VD, VD)].rearrange("(t p) d -> p t d", p=P),
                        osb[:, :, :]).then_inc(o_st, 16)

        def act_sumsq_x(e, t):
            e.wait_ge(x_ld[t % 3], 16 * (t // 3 + 1))
            e.activation(junk[0:rows(t), :], xt[t % 3][0:rows(t), :], ACT.Square,
                         accum_out=sst[0:rows(t), t % 4, 0:1]).then_inc(sumsq_x, 1)

        def act_phase1(e):
            e.wait_ge(sst_set, 1)
            for t in range(3):
                if t:
                    e.wait_ge(sumsq_x, t)
                act_sumsq_x(e, t)
                act_split_w(e, 0, 0, t)
            for t in range(TT):
                for half in range(2):
                    e.wait_ge(tr_x, 2 * t + half + 1)
                    e.activation(act_hi[:, 4 * half:4 * half + 4, t * P:t * P + rows(t)],
                                 PS[:, 2 * (t % 2) + half, :].rearrange("p (a b) -> p a b", b=P)[:, :, 0:rows(t)],
                                 ACT.Copy).then_inc(hi_x, 1)
                if t + 3 < TT:
                    e.wait_ge(sumsq_x, t + 3)
                    act_sumsq_x(e, t + 3)
                if t >= 1:
                    act_evac_projection(e, 0, 0, t - 1, 0)
                if t >= 6:
                    act_split_w(e, 1, 1, t - 6)
                if t == 6:
                    act_evac_qk(e, 0, 0, 0, 0)
            act_evac_projection(e, 0, 0, TT - 1, 0)
            act_evac_qk(e, 0, 0, 1, 2)
            e.wait_ge(lam_step, 1)
            e.activation(lam_s[:, 2:4], lam_s[:, 0:2], ACT.Exp).then_inc(lam_step, 1)
            with e.Fori(0, NH // 2 - 1) as i:
                for slot in range(2):
                    act_head(e, i * 2 + slot, slot, True, True, i + slot)
            act_head(e, NH - 2, 0, True, False, NH // 2 - 1)
            act_head(e, NH - 1, 1, False, False, 0)

        def dve_normalize_x(e, t):
            e.wait_ge(rstd_x, t + 1)
            e.scalar_tensor_tensor(out=xt[t % 3][0:rows(t), :], in0=xt[t % 3][0:rows(t), :],
                                   scalar=rst[0:rows(t), t % 4, 0:1], in1=gain_x[0:rows(t), :],
                                   op0=ALU.mult, op1=ALU.mult).then_inc(xn_x, 1)

        def dve_tail_x(e, t):
            for half in range(2):
                e.wait_ge(hi_x, 2 * t + half + 1)
                src = PS[:, 2 * (t % 2) + half, :].rearrange("p (a b) -> p a b", b=P)[:, :, 0:rows(t)]
                e.tensor_tensor(act_lo[:, 4 * half:4 * half + 4, t * P:t * P + rows(t)], src,
                                act_hi[:, 4 * half:4 * half + 4, t * P:t * P + rows(t)].bitcast(F32),
                                ALU.subtract).then_inc(lo_x, 1)

        def dve_sumsq_qk(e, step, n, slot, g):
            e.wait_ge(pj_free, n * TT + 3 * g + 3 + 2)
            src = raw[slot][:, 3 * g:3 * g + 3, 0:2 * VD]
            step(e.tensor_tensor(sq[:, :, :], src, src, ALU.mult))
            e.tensor_reduce(ss[:, 0:12].rearrange("p (t c) -> p t c", t=3),
                            sq[:, :, :].rearrange("p t (c d) -> p t c d", d=HD), AX.X, ALU.add).then_inc(sumsq_qk, 1)

        def dve_scale_qk(e, n, slot, g):
            e.wait_ge(rstd_qk, n * 3 + g + 1)
            src = raw[slot][:, 3 * g:3 * g + 3, 0:2 * VD].rearrange("p t (c d) -> p t c d", d=HD)
            e.tensor_tensor(src, src, rs[:, 0:12].rearrange("p (t c) -> p t c", t=3).unsqueeze(3)
                            .to_broadcast([P, 3, 4, HD]), ALU.mult).then_inc(scaled_qk, 1)

        def dve_max(e, step, h, s):
            e.wait_ge(s_full, h * QT + s + 1)
            n = (s + 1) * P
            diag = scores_ps[:, :, s * P:n]
            step(e.tensor_tensor(diag, diag, causal[:, :].unsqueeze(1).to_broadcast([P, 2, P]), ALU.add))
            step(e.tensor_reduce(row_max[:, s % 2, :], scores_ps[:, :, 0:n], AX.X, ALU.max))
            e.tensor_scalar(negm[:, s % 2, :], row_max[:, s % 2, :], -SCALE, None, ALU.mult).then_inc(negm_ready, 1)

        def dve_probs(e, step, h, s):
            e.wait_ge(exp_done, h * QT + s + 2)
            n = (s + 1) * P
            b = s % 2
            step(e.reciprocal(rden[:, b, :], den[:, b, :]))
            e.tensor_scalar(E[b][:, 0, 0:n], E[b][:, 0, 0:n], rden[:, b, 0:1], None, ALU.mult)
            step(e.tensor_scalar(rden[:, b, 1:2], rden[:, b, 1:2], neglam[:, 0:1], None, ALU.mult))
            e.scalar_tensor_tensor(out=E[b][:, 0, 0:n], in0=E[b][:, 1, 0:n], scalar=rden[:, b, 1:2],
                                   in1=E[b][:, 0, 0:n], op0=ALU.mult, op1=ALU.add).then_inc(p_ready, 1)

        def dve_head(e, step, h, slot, proj):
            for s in range(TT):
                if s >= 1:
                    dve_probs(e, step, h, s - 1)
                if s < QT:
                    dve_max(e, step, h, s)
                if s == 0:
                    dve_sumsq_qk(e, step, h, slot, 2)
                if s == 1:
                    dve_scale_qk(e, h, slot, 2)
                if proj and s in (3, 6):
                    dve_sumsq_qk(e, step, h + 1, 1 - slot, s // 3 - 1)
                if proj and s in (4, 7):
                    dve_scale_qk(e, h + 1, 1 - slot, s // 3 - 1)

        DVE_HEAD = 4 * QT + 3

        def dve_phase1(e, step):
            e.memset(sst[:, :, :], 1.0).then_inc(sst_set, 1)
            for slot in range(2):
                step(e.memset(raw[slot][NSAMP:P, QT, :], 0.0))
            e.wait_ge(gain_x_ld, 16)
            dve_normalize_x(e, 0)
            dve_normalize_x(e, 1)
            for t in range(TT):
                dve_tail_x(e, t)
                if t + 2 < TT:
                    dve_normalize_x(e, t + 2)
                if t in (3, 6):
                    dve_sumsq_qk(e, step, 0, 0, t // 3 - 1)
                if t in (4, 7):
                    dve_scale_qk(e, 0, 0, t // 3 - 1)
            e.wait_ge(lam_ld, 64)
            lam_v = sq[:, 0, :].rearrange("p (a d) -> p a d", d=HD)
            step(e.tensor_tensor(lam_v[:, 0:2, :], lam_v[:, 0:2, :], lam_v[:, 2:4, :], ALU.mult))
            e.tensor_reduce(lam_s[:, 0:2], lam_v[:, 0:2, :], AX.X, ALU.add).then_inc(lam_step, 1)
            e.wait_ge(lam_step, 2)
            step(e.tensor_tensor(neglam[:, :], lam_s[:, 3:4], lam_s[:, 2:3], ALU.subtract))
            step(e.tensor_scalar(neglam[:, :], neglam[:, :], -LAMBDA_INIT, None, ALU.add))
            e.wait_ge(consts_step, 1)
            step(e.tensor_scalar(rowi[:, 2 * NS:2 * NS + 1], rowi[:, 0:1], NS, None, ALU.bitwise_and))
            step(e.tensor_scalar(rowi[:, 0:NS], rowi[:, 0:NS], NS - 1, None, ALU.bitwise_and))
            step(e.tensor_scalar(coef[:, :], rowi[:, 2 * NS:2 * NS + 1], 1.0 / NS, None, ALU.mult))
            step(e.tensor_tensor(new_mask[:, :], rowi[:, 0:NS], rowi[:, NS:2 * NS], ALU.is_lt))
            step(e.tensor_scalar(new_mask[:, :], new_mask[:, :], NEG, None, ALU.mult))
            step(e.tensor_scalar(lam_s[:, 0:1], neglam[:, :], -1.0, None, ALU.add))
            step(e.tensor_tensor(coef[:, :], coef[:, :], lam_s[:, 0:1], ALU.mult))
            step(e.tensor_scalar(coef[:, :], coef[:, :], 1.0, None, ALU.add))
            n0 = step.n
            with e.Fori(0, NH // 2 - 1) as i:
                step.n = n0 + i * (2 * DVE_HEAD)
                for slot in range(2):
                    dve_head(e, step, i * 2 + slot, slot, True)
            step.n = n0 + (NH // 2 - 1) * 2 * DVE_HEAD
            dve_head(e, step, NH - 2, 0, True)
            assert step.n == n0 + (NH - 1) * DVE_HEAD, (step.n - n0, DVE_HEAD)
            dve_head(e, step, NH - 1, 1, False)

        def pool_rstd(e, step, dst, src, width, n):
            step(e.tensor_tensor(dst, src, inv_n[n][:, 0:width], ALU.mult))
            step(e.tensor_tensor(dst, dst, eps_t[0:dst.shape[0], 0:width], ALU.add))
            return e.tensor_tensor(dst, dst, neghalf[0:dst.shape[0], 0:width], ALU.pow)

        def pool_rstd_qk(e, step, n, g):
            e.wait_ge(sumsq_qk, n * 3 + g + 1)
            pool_rstd(e, step, rs[:, :], ss[:, :], 12, HD).then_inc(rstd_qk, 1)

        def pool_gain_qk(e, n, slot, g):
            e.wait_ge(scaled_qk, n * 3 + g + 1)
            part = raw[slot][:, 3 * g:3 * g + 3, 0:2 * VD]
            e.tensor_tensor(part, part, gain_qk[:, :].unsqueeze(1).to_broadcast([P, 3, 2 * VD]),
                            ALU.mult).then_inc(gained_qk, 1)

        def pool_split_w(e, m, slot, piece):
            a, b = SPLITS[piece]
            e.wait_ge(w_head, m * 3 + piece + 1)
            e.tensor_tensor(w_lo[slot][:, a:b, :, :], w_raw[:, a:b, :, :],
                            w_hi[slot][:, a:b, :, :].bitcast(F32), ALU.subtract).then_inc(w_tail, 1)

        def pool_head(e, step, h, slot, proj, split):
            for s in range(TT):
                if s == 0:
                    pool_rstd_qk(e, step, h, 2)
                    if split:
                        pool_split_w(e, h + 2, slot, 0)
                if s == 1:
                    pool_gain_qk(e, h, slot, 2)
                if proj and s in (4, 7):
                    pool_gain_qk(e, h + 1, 1 - slot, s // 3 - 1)
                if proj and s in (3, 6):
                    pool_rstd_qk(e, step, h + 1, s // 3 - 1)
                    if split:
                        pool_split_w(e, h + 2, slot, s // 3)

        def pool_constants(e, step):
            step(e.memset(ident[:, :], 0.0))
            step(e.memset(neghalf[:, :], -0.5))
            step(e.memset(eps_t[:, :], EPS))
            for n, tile in inv_n.items():
                step(e.memset(tile[:, :], 1.0 / n))
            e.affine_select(out=ident[:, :], in_=ident[:, :], compare_op=ALU.not_equal, fill=1.0, base=0,
                            pattern=[[-1, P]], channel_multiplier=1).then_inc(consts, 1)
            for s in (pj_free, fm_free, fm_full):
                e.sem_inc(s, 2)
            for s in (kv_st[0], kv_st[1], o_st, os_st[0], os_st[1], st_st, os_full, os_copied, pt_free,
                      exp_done, pts_copied):
                e.sem_inc(s, 1)
            step(e.memset(causal[:, :], 0.0))
            step(e.affine_select(out=causal[:, :], in_=causal[:, :], compare_op=ALU.is_ge, fill=NEG, base=0,
                                 pattern=[[-1, P]], channel_multiplier=1))
            step(e.memset(kT_s[:, NH, :], 0.0))
            step(e.memset(pick[:, :], 0.0))
            for c in range(2):
                v = pick[:, 0:NH * NS].rearrange("p (h q) -> p h q", h=NH)
                step(e.affine_select(out=v, in_=v, compare_op=ALU.not_equal, fill=1.0, base=-NS * c,
                                     pattern=[[-2 * NS, NH], [-1, NS]], channel_multiplier=1))
            step(e.iota(rowi[:, 0:NS], pattern=[[0, NS]], base=0, channel_multiplier=1))
            e.iota(rowi[:, NS:2 * NS], pattern=[[1, NS]], base=0, channel_multiplier=0).then_inc(consts_step, 1)
            e.wait_ge(consts_step, 1)

        def pool_phase1(e, step):
            for t in range(TT):
                e.wait_ge(sumsq_x, t + 1)
                pool_rstd(e, step, rst[:, t % 4, 0:1], sst[:, t % 4, 0:1], 1, D).then_inc(rstd_x, 1)
                if t < 3:
                    pool_split_w(e, 0, 0, t)
                if t == 6:
                    e.wait_ge(gain_ld, 64)
                    pool_rstd_qk(e, step, 0, 0)
                if t == 7:
                    pool_gain_qk(e, 0, 0, 0)
            pool_split_w(e, 1, 1, 0)
            pool_rstd_qk(e, step, 0, 1)
            pool_gain_qk(e, 0, 0, 1)
            for piece in range(1, 3):
                pool_split_w(e, 1, 1, piece)
            n0 = step.n
            with e.Fori(0, NH // 2 - 1) as i:
                step.n = n0 + i * 12
                for slot in range(2):
                    pool_head(e, step, i * 2 + slot, slot, True, True)
            step.n = n0 + 6 * (NH - 2)
            pool_head(e, step, NH - 2, 0, True, False)
            pool_head(e, step, NH - 1, 1, False, False)

        w_in_v = w_in[0].rearrange("(kt p) n -> p kt n", p=P)

        def sp_load_w0(e, piece):
            a, b = SPLITS[piece]
            for x in range(3):
                e.dma_start(w_raw[:, a:b, x, :], w_in_v[:, a:b, x * D:x * D + VD]).then_inc(w0_ld[piece], 16)

        def sp_load_w(e, m):
            for x in range(3):
                e.dma_start(w_raw[:, :, x, :], w_in_v[:, :, bass.ds(m * VD + x * D, VD)]).then_inc(w_ld, 16)

        def sp_store_kv(e, h, slot):
            e.wait_ge(gained_qk, h * 3 + 3)
            for dst_p, dst_s, x in ((k_prompt, k_sample, 1), (v_prompt, v_sample, 2)):
                e.dma_start(dst_p[0, 0][:, bass.ds(h, 1), :].rearrange("(t p) a d -> p t (a d)", p=P),
                            raw[slot][:, 0:QT, x * VD:(x + 1) * VD]).then_inc(kv_st[slot], 16)
                e.dma_start(dst_s[0][:, :, bass.ds(h, 1), :].rearrange("b q a d -> (b q) (a d)"),
                            raw[slot][0:NSAMP, QT, x * VD:(x + 1) * VD]).then_inc(kv_st[slot], 16)

        def sp_load_x(e, t):
            if t >= 3:
                e.wait_ge(tr_x, 2 * (t - 3) + 2)
            src = x_prompt[0, t * P:(t + 1) * P, :] if t < QT else x_sample.rearrange("b q d -> (b q) d")
            e.dma_start(xt[t % 3][0:rows(t), :], src).then_inc(x_ld[t % 3], 16)

        def sp_phase1(e):
            sp_load_x(e, 0)
            e.dma_start(gain_x[:, :], norm_mix[0:1, :].to_broadcast([P, D])).then_inc(gain_x_ld, 16)
            sp_load_w0(e, 0)
            sp_load_x(e, 1)
            sp_load_w0(e, 1)
            sp_load_w0(e, 2)
            sp_load_x(e, 2)
            for c in range(2):
                e.dma_start(gain_qk[:, c * HD:(c + 1) * HD], q_norm[0, c:c + 1, :].to_broadcast([P, HD])).then_inc(gain_ld, 16)
                e.dma_start(gain_qk[:, VD + c * HD:VD + (c + 1) * HD], k_norm[0, c:c + 1, :].to_broadcast([P, HD])).then_inc(gain_ld, 16)
            e.dma_start(pgt[:, :], page_table.rearrange("b n -> (b n)").rearrange("(a n) -> a n", a=1)
                        ).then_inc(pg_ld, 16)
            for t in range(3, TT):
                sp_load_x(e, t)
            e.wait_ge(w_tail, 3)
            sp_load_w(e, 1)
            e.wait_ge(sumsq_qk, 2)
            for i, v in enumerate((lambda_q1, lambda_q2, lambda_k1, lambda_k2)):
                e.dma_start(sq[:, 0, i * HD:(i + 1) * HD], v[0:1, :].to_broadcast([P, HD])).then_inc(lam_ld, 16)
            with e.Fori(0, NH // 2 - 1) as i:
                for slot in range(2):
                    e.wait_ge(w_tail, (i * 2 + slot) * 3 + 6)
                    sp_load_w(e, i * 2 + slot + 2)
                    sp_store_kv(e, i * 2 + slot, slot)
            sp_store_kv(e, NH - 2, 0)
            sp_store_kv(e, NH - 1, 1)

        HALF_PG = NPG // 2
        r = Region(X0, X_END - 20480)
        k_pg = [r(f"k_pg{j}", [P, NH * VD]) for j in range(NPG)]
        v_pg = [r(f"v_pg{j}", [P, NH * VD]) for j in range(NPG - 1)]
        assert r.at <= raw_at[0]
        QW = P + 2 * NS
        q_blk = [r(f"q_blk{i}", [P, NH * QW]) for i in range(2)]
        assert r.at <= raw_at[1]
        v_pg.append(r(f"v_pg{NPG - 1}", [P, NH * VD]))
        ktp = [r(f"ktp{i}", [P, HALF_PG * PAGE]) for i in range(2)]
        es = [r(f"es{i}", [P, PASTK + NS]) for i in range(2)]
        s_new = r("s_new", [P, 2, NS])
        pts = [r(f"pts{i}", [P, 4, NH * NS]) for i in range(3)]
        v_new = [r(f"v_new{i}", [NS, NH * VD]) for i in range(2)]
        os_sb = [r(f"os_sb{i}", [NSAMP, D]) for i in range(2)]
        pick_r = [r(f"pick_r{i}", [P, P]) for i in range(2)]
        smax = r("smax", [P, 2, 4])
        snm = r("snm", [P, 2, 1])
        sden = r("sden", [P, 2, 4])
        B_KT, B_S, B_NEW, B_PTS, B_OS = 0, 2, 4, 5, 6

        pg_ld = sem("pg_ld")
        k_ld = [sem(f"k_ld{j}") for j in range(NPG)]
        v_ld = [sem(f"v_ld{j}") for j in range(NPG)]
        vn_ld = [sem(f"vn_ld{i}") for i in range(2)]
        qb_ready = sem("qb_ready")
        kt_full = sem("kt_full")
        kt_copied = sem("kt_copied")
        sc_half = sem("sc_half")
        sc_new = sem("sc_new")
        snm_ready = sem("snm_ready")
        es_done = sem("es_done")
        pick_done = sem("pick_done")
        pts_full = sem("pts_full")
        pts_copied = sem("pts_copied")
        v_half = sem("v_half")
        os_full = sem("os_full")
        os_copied = sem("os_copied")
        os_st = [sem(f"os_st{i}") for i in range(2)]

        KT_PER = 2 * NH
        PTS_GROUPS = [list(range(4)), list(range(4, 8)), [8]]

        def phase1_over(e):
            e.wait_ge(b7_free, b_use(NH - 1, False, ("o", TT - 1)) + 1)
            e.wait_ge(o_st, NH * 16 + 1)
            for i in range(2):
                e.wait_ge(kv_st[i], NH // 2 * 64 + 1)

        def pe_keys(e, b, par):
            e.wait_ge(qb_ready, b + 1)
            stationary = [q_blk[par][:, h * P:(h + 1) * P] for h in range(NH)]

            def scores(idx):
                half, h = divmod(idx, NH)
                if h == 0:
                    e.wait_ge(es_done, b)
                e.wait_ge(kt_copied, b * KT_PER + idx + 1)
                ins = e.matmul(PS[:, B_S + half, :], stationary[h], ktp[idx % 2][:, :],
                               start=h == 0, stop=h == NH - 1)
                ins.then_inc(sc_half, 1)

            for idx in range(KT_PER):
                half, h = divmod(idx, NH)
                if h == 0:
                    for j in range(HALF_PG):
                        e.wait_ge(k_ld[HALF_PG * half + j], b * 16 + 16)
                e.wait_ge(kt_copied, b * KT_PER + idx - 1 if idx else b * KT_PER)
                for j in range(HALF_PG):
                    ins = e.transpose(PS[:, B_KT + idx % 2, j * PAGE:(j + 1) * PAGE],
                                      k_pg[HALF_PG * half + j][:, h * VD:(h + 1) * VD], ident[:, :])
                ins.then_inc(kt_full, 1)
                if idx >= 1:
                    scores(idx - 1)
            for h in range(NH):
                ins = e.matmul(PS[:, B_NEW, 0:P], stationary[h],
                               kT_s[:, h:h + 2, :].rearrange("p a b -> p (a b)"),
                               start=h == 0, stop=h == NH - 1)
            ins.then_inc(sc_new, 1)
            scores(KT_PER - 1)

        def pe_pages(e, b, par):
            e.wait_ge(pick_done, b + 1)

            def transposed(g):
                e.wait_ge(pts_copied, b * 3 + g + 1)
                for i, j in enumerate(PTS_GROUPS[g]):
                    m = PAGE if j < NPG else NS
                    ins = e.matmul(PS[0:m, B_PTS, i * P:(i + 1) * P], es[par][:, j * PAGE:j * PAGE + m],
                                   pick_r[par][:, :], start=True, stop=True)
                ins.then_inc(pts_full, 1)

            transposed(0)
            e.wait_ge(os_copied, b + 1)
            for g in range(3):
                e.wait_ge(pts_copied, b * 3 + g + 2)
                if g + 1 < 3:
                    transposed(g + 1)
                for i, j in enumerate(PTS_GROUPS[g]):
                    m = PAGE if j < NPG else NS
                    if j < NPG:
                        e.wait_ge(v_ld[j], b * 16 + 16)
                    else:
                        e.wait_ge(vn_ld[par], (b - par) * 8 + 16)
                    v = v_pg[j] if j < NPG else v_new[par]
                    for n in range(2):
                        ins = e.matmul(PS[0:NSAMP, B_OS + n, :], pts[g][0:m, i, :],
                                       v[0:m, n * 512:(n + 1) * 512], start=j == 0, stop=j == NPG)
                if g == 0:
                    ins.then_inc(v_half, 1)
            ins.then_inc(os_full, 1)

        def for_sequences(e, first, both, last):
            first(0, 0)
            with e.Fori(0, (NB - 2) // 2) as i:
                both(i * 2 + 1, 1)
                both(i * 2 + 2, 0)
            both(NB - 1, 1)
            last(NB - 1, 1)

        def pe_phase2(e):
            e.wait_ge(b7_free, b_use(NH - 1, False, ("o", TT - 1)) + 1)
            def both(b, par):
                pe_keys(e, b, par)
                pe_pages(e, b - 1, 1 - par)

            for_sequences(e, lambda b, par: pe_keys(e, b, par), both, lambda b, par: pe_pages(e, b, par))

        def act_store(e, b, par, h):
            e.dma_start(o_dram[bass.ds(SEQ + b * NS, NS), h * VD:(h + 1) * VD],
                        os_sb[par][h * NS:(h + 1) * NS, h * VD:(h + 1) * VD]).then_inc(os_st[par], 16)

        def act_keys(e, b, par, store=None):
            for idx in range(KT_PER):
                if store is not None and idx % 2:
                    store(idx // 2)
                e.wait_ge(kt_full, b * KT_PER + idx + 1)
                if idx >= 2:
                    e.wait_ge(sc_half, b * KT_PER + idx - 1)
                else:
                    e.wait_ge(sc_half, b * KT_PER)
                e.activation(ktp[idx % 2][:, :], PS[:, B_KT + idx % 2, :], ACT.Copy).then_inc(kt_copied, 1)
            e.wait_ge(snm_ready, b + 1)
            e.activation(es[par][:, 0:PASTK], PS[:, B_S:B_S + 2, :].rearrange("p a b -> p (a b)"), ACT.Exp,
                         bias=snm[:, par, :], scale=SCALE, accum_out=sden[:, par, 0:1])
            e.activation(es[par][:, PASTK:PASTK + NS], s_new[:, par, :], ACT.Exp,
                         bias=snm[:, par, :], scale=SCALE, accum_out=sden[:, par, 1:2]).then_inc(es_done, 1)

        def act_pages(e, b, par):
            e.wait_ge(os_st[par], (b - par) * (8 * NH) + 1)
            e.wait_ge(os_full, b + 2)
            e.activation(os_sb[par][:, :], PS[0:NSAMP, B_OS:B_OS + 2, :].rearrange("p a b -> p (a b)"),
                         ACT.Copy).then_inc(os_copied, 1)

        def act_phase2(e):
            def both(b, par):
                e.wait_ge(os_copied, b)
                act_keys(e, b, par, lambda h: act_store(e, b - 2, par, h))
                act_pages(e, b - 1, 1 - par)

            e.wait_ge(kv_st[1], NH // 2 * 64 + 1)
            act_keys(e, 0, 0)
            fm_head(e, 0, 0)
            act_keys(e, 1, 1)
            act_pages(e, 0, 0)
            with e.Fori(0, (NB - 2) // 2) as i:
                both(i * 2 + 2, 0)
                both(i * 2 + 3, 1)
            act_pages(e, NB - 1, 1)
            e.wait_ge(os_copied, NB + 1)
            for b in (NB - 2, NB - 1):
                for h in range(NH):
                    act_store(e, b, b % 2, h)

        def dve_keys(e, step, b, par):
            e.wait_ge(sc_new, b + 1)
            e.tensor_tensor(s_new[:, par, :], PS[:, B_NEW, bass.ds(b * NS, NS)], new_mask[:, :],
                            ALU.add).then_inc(dve_step, 1)
            e.wait_ge(sc_half, b * KT_PER + KT_PER)
            e.tensor_reduce(smax[:, par, 0:1], PS[:, B_S:B_S + 2, :].rearrange("p a b -> p (a b)"), AX.X,
                            ALU.max).then_inc(dve_step, 1)
            step.n = step.n + 2
            e.wait_ge(dve_step, step.n)
            step(e.tensor_reduce(smax[:, par, 1:2], s_new[:, par, :], AX.X, ALU.max))
            step(e.tensor_tensor(smax[:, par, 2:3], smax[:, par, 0:1], smax[:, par, 1:2], ALU.max))
            e.tensor_scalar(snm[:, par, :], smax[:, par, 2:3], -SCALE, None, ALU.mult).then_inc(snm_ready, 1)
            e.wait_ge(es_done, b + 1)
            step(e.tensor_tensor(sden[:, par, 2:3], sden[:, par, 0:1], sden[:, par, 1:2], ALU.add))
            step(e.reciprocal(sden[:, par, 3:4], sden[:, par, 2:3]))
            step(e.tensor_tensor(sden[:, par, 3:4], sden[:, par, 3:4], coef[:, :], ALU.mult))
            e.tensor_scalar(pick_r[par][:, :], pick[:, :], sden[:, par, 3:4], None, ALU.mult).then_inc(pick_done, 1)

        DVE_KEYS = 7

        def dve_pages(e, b):
            for g, pages in enumerate(PTS_GROUPS):
                m = PAGE if pages[0] < NPG else NS
                e.wait_ge(pts_full, b * 3 + g + 1)
                e.wait_ge(os_full, b + 1)
                e.tensor_copy(pts[g][0:m, 0:len(pages), :],
                              PS[0:m, B_PTS, :].rearrange("p (a b) -> p a b", b=P)[:, 0:len(pages), 0:NH * NS]
                              ).then_inc(pts_copied, 1)

        def dve_phase2(e, step):
            n0 = step.n
            dve_keys(e, step, 0, 0)
            with e.Fori(0, (NB - 2) // 2) as i:
                step.n = n0 + DVE_KEYS + i * (2 * DVE_KEYS)
                for k in range(2):
                    dve_pages(e, i * 2 + k)
                    dve_keys(e, step, i * 2 + k + 1, 1 - k)
            step.n = n0 + DVE_KEYS * (NB - 1)
            dve_pages(e, NB - 2)
            dve_keys(e, step, NB - 1, 1)
            dve_pages(e, NB - 1)

        def pool_phase2(e, step):
            e.wait_ge(b7_free, b_use(NH - 2, True, ("o", TT - 1)) + 1)
            e.wait_ge(kv_st[0], NH // 2 * 64 + 1)
            for par in range(2):
                step(e.memset(q_blk[par][:, :], 0.0))
            e.wait_ge(b7_free, b_use(NH - 1, False, ("k", 2)) + 1)
            for b in range(NB):
                if b >= 2:
                    e.wait_ge(sc_new, b - 1)
                    e.wait_ge(sc_half, (b - 1) * KT_PER)
                for c in range(2):
                    dst = q_blk[b % 2][:, :].rearrange("p (h x) -> p h x", x=QW)
                    ins = e.tensor_copy(dst[c * HD:(c + 1) * HD, :, c * NS:(c + 1) * NS],
                                        qT_s[c * HD:(c + 1) * HD, :, b * NS:(b + 1) * NS])
                    if c == 0:
                        step(ins)
                ins.then_inc(qb_ready, 1)
                e.wait_ge(qb_ready, b + 1)
            fm_tail(e, 0, 0)

        def sp_load_pages(e, b, tiles, sems, cache, pages, used=None):
            for j in pages:
                page = e.value_load(pgt[0:1, bass.ds(b * NPG + j, 1)], min_val=0, max_val=NPHYS - 1)
                if j == pages[0] and used is not None:
                    e.wait_ge(*used)
                    e.wait_ge(pg_ld, 16)
                e.dma_start(tiles[j][:, :], cache[0, bass.ds(page, 1)].rearrange("a p h d -> (a p) (h d)")
                            ).then_inc(sems[j], 16)

        def sp_load_values(e, b, par):
            for half in range(2):
                used = None if after_first(b) is False else (v_half, b) if half == 0 else (os_full, b + 1)
                sp_load_pages(e, b, v_pg, v_ld, cache_v, range(half * HALF_PG, (half + 1) * HALF_PG), used)
            sp_load_new_values(e, b, par)

        def sp_load_new_values(e, b, par):
            e.dma_start(v_new[par][:, :], v_sample[0, bass.ds(b, 1)].rearrange("a q h d -> (a q) (h d)")
                        ).then_inc(vn_ld[par], 16)

        def sp_load_keys(e, b):
            for half in range(2):
                sp_load_pages(e, b, k_pg, k_ld, cache_k, range(half * HALF_PG, (half + 1) * HALF_PG),
                              (kt_full, (b - 1) * KT_PER + (half + 1) * NH))

        def after_first(j):
            return not (isinstance(j, int) and j == 0)

        def sp_phase2(e):
            e.wait_ge(pg_ld, 16)
            e.wait_ge(pj_full, NH * TT)
            sp_load_pages(e, 0, k_pg, k_ld, cache_k, range(NPG))
            sp_load_pages(e, 0, v_pg, v_ld, cache_v, range(NPG - 1))
            phase1_over(e)
            sp_load_pages(e, 0, v_pg, v_ld, cache_v, [NPG - 1])
            sp_load_new_values(e, 0, 0)
            sp_load_keys(e, 1)
            sp_prefetch_phase3(e)
            with e.Fori(0, (NB - 2) // 2) as i:
                for k in range(2):
                    sp_load_keys(e, i * 2 + k + 2)
                    sp_load_values(e, i * 2 + k + 1, 1 - k)
            sp_load_values(e, NB - 1, 1)

        N_U, N_GP, N_GA, N_PL, N_PB, N_AB, N_UP = 0, KT, 2 * KT, 3 * KT, 4 * KT, 5 * KT, 6 * KT
        STREAM = X_END - 5 * fit(KT, P)
        r = Region(STREAM, X_END)
        fw_raw = r("fw_raw", [P, KT, P])
        fw_hi, fw_lo, fw_at = [], [], []
        for i in range(2):
            fw_at.append(r.at)
            fw_hi.append(r(f"fw_hi{i}", [P, KT, P], F32R))
            fw_lo.append(r(f"fw_lo{i}", [P, KT, P], F32R))
        R2 = X0
        R2U = R2 + R1_BYTES // 2
        R3 = R2 + R1_BYTES
        dT = at("dT", [P, KT, TOK], F32, R2)
        oT = at("oT", [P, KT, TOK], F32, R2)
        m_hi = at("m_hi", [P, KT, TOK], F32R, R2)
        sig_a = at("sig_a", [P, KT, TOK], F32, R2U)
        m_lo = at("m_lo", [P, KT, TOK], F32R, R2U)
        sig_p = at("sig_p", [P, KT, TOK], F32, R3)
        UE = BUF + SEQ + NB * (BUF + NS)
        r = Region(R2U, R3)
        u_ext = [r(f"u_ext{i}", [P, UE]) for i in range(2)]
        u_sum = [r(f"u_sum{i}", [P, UE]) for i in range(2)]
        u_col = [r(f"u_col{i}", [P, NSAMP + BUF]) for i in range(2)]
        sp_rows = r("sp_rows", [NB * BUF, D])
        u_rows = r("u_rows", [NSAMP + BUF, D])
        r = Region(fw_at[1], pgt_at)
        gain_rows = r("gain_rows", [2 * KT, P])
        conv_rows = [r(f"conv_rows{i}", [4 * FT, P]) for i in range(2)]
        ffn_rows = r("ffn_rows", [P, 6, P])
        r = Region(R3 + fit(KT, TOK), STREAM)
        o_tile = r("o_tile", [P, D])
        o_sq = r("o_sq", [P, D])
        r = Region(late_at, R1)
        conv_c = r("conv_c", [P, 4, 2 * FT])
        ffn_pre = r("ffn_pre", [P, 6, 8, NB * 2])
        st_col = [r(f"st_col{i}", [P, 4, 2 + 2 * NB]) for i in range(2)]

        fw_ld = sem("fw_ld")
        fw_head = sem("fw_head")
        fw_tail = sem("fw_tail")
        fm_full = sem("fm_full")
        fm_free = sem("fm_free")
        prep_ld = sem("prep_ld")
        sp_ld = sem("sp_ld")
        prep_full = sem("prep_full")
        prep_done = sem("prep_done")
        zeros_set = sem("zeros_set")
        pre_full = sem("pre_full")
        pre_copied = sem("pre_copied")
        u_ready = sem("u_ready")
        d_done = sem("d_done")
        ucol_ready = sem("ucol_ready")
        ur_full = sem("ur_full")
        ur_copied = sem("ur_copied")
        ur_st = sem("ur_st")
        d_head = sem("d_head")
        d_tail = sem("d_tail")
        po_head = sem("po_head")
        po_tail = sem("po_tail")
        o_ld = sem("o_ld")
        sumsq_o = sem("sumsq_o")
        rstd_o = sem("rstd_o")
        scaled_o = sem("scaled_o")
        o_tr = sem("o_tr")
        ot_done = sem("ot_done")
        o_head = sem("o_head")
        o_tail = sem("o_tail")
        m_sum = sem("m_sum")
        m_head = sem("m_head")
        m_tail = sem("m_tail")

        def phase2_over(e):
            e.wait_ge(os_full, NB + 1)
            for i in range(2):
                e.wait_ge(os_st[i], NB // 2 * NH * 16 + 1)

        def fm_done(e, n):
            e.wait_ge(fm_full, n + 3)

        def fm_parts(slot):
            b = 3 * slot
            return ((PS[:, b:b + 2, 0:CW], 0, 2 * CW), (PS[:, b + 2:b + 3, 0:TOK - 2 * CW], 2 * CW, TOK))

        def cols(tile, lo, hi):
            v = tile[:, lo:hi]
            return v.rearrange("p (a b) -> p a b", a=2 if lo == 0 else 1)

        def flat(tile, m):
            return tile[:, bass.ds(m, 1), :].rearrange("p a t -> p (a t)")

        def fm_load(e, n, src, also_wait=None):
            if not (isinstance(n, int) and n == 0):
                e.wait_ge(fw_tail, n)
            if also_wait is not None:
                also_wait()
            e.dma_start(fw_raw[:, 0:src.shape[1], :], src).then_inc(fw_ld, 16)

        def fm_head(e, n, slot, kts=KT):
            e.wait_ge(fw_ld, n * 16 + 16)
            fm_done(e, n - 2)
            e.activation(fw_hi[slot][:, 0:kts, :], fw_raw[:, 0:kts, :], ACT.Copy).then_inc(fw_head, 1)

        def fm_tail(e, n, slot, kts=KT):
            e.wait_ge(fw_head, n + 1)
            e.tensor_tensor(fw_lo[slot][:, 0:kts, :], fw_raw[:, 0:kts, :],
                            fw_hi[slot][:, 0:kts, :].bitcast(F32), ALU.subtract).then_inc(fw_tail, 1)

        def pe_fm_tile(e, n, slot, hi, lo, k0=0, kts=KT, ready=None):
            e.wait_ge(fw_tail, n + 1)
            e.wait_ge(fm_free, n + 1)
            for kt in range(kts):
                if ready is not None:
                    e.wait_ge(ready, k0 + kt + 1)
                for w, x, first, last in ((fw_hi, hi, True, False), (fw_hi, lo, False, False), (fw_lo, hi, False, True)):
                    for c, (c0, cw) in enumerate(CHUNKS):
                        ins = e.matmul(PS[:, 3 * slot + c, 0:cw], w[slot][:, kt, :],
                                       x[:, k0 + kt, c0:c0 + cw],
                                       start=first and kt == 0, stop=last and kt == kts - 1)
            ins.then_inc(fm_full, 1)

        def pe_fm_tile_by_chunk(e, n, slot, hi, lo, before_chunk):
            e.wait_ge(fw_tail, n + 1)
            e.wait_ge(fm_free, n + 1)
            for c, (c0, cw) in enumerate(CHUNKS):
                before_chunk(c)
                for kt in range(KT):
                    for w, x, first, last in ((fw_hi, hi, True, False), (fw_hi, lo, False, False), (fw_lo, hi, False, True)):
                        ins = e.matmul(PS[:, 3 * slot + c, 0:cw], w[slot][:, kt, :], x[:, kt, c0:c0 + cw],
                                       start=first and kt == 0, stop=last and kt == KT - 1)
            ins.then_inc(fm_full, 1)

        def pairs(e, n0, body):
            with e.Fori(0, KT // 2) as i:
                for slot in range(2):
                    body(n0 + i * 2 + slot, i * 2 + slot, slot)

        def pe_o_transposes(e, idx, n_rows):
            e.wait_ge(scaled_o, idx + 1)
            for half in range(2):
                e.wait_ge(ot_done, idx * 2)
                for j in range(4):
                    h = 4 * half + j
                    ins = e.transpose(PS[:, 6 + half, j * P:j * P + n_rows], o_tile[0:n_rows, h * P:(h + 1) * P],
                                      ident[0:n_rows, 0:n_rows])
                ins.then_inc(o_tr, 1)

        def pe_phase3(e):
            e.wait_ge(prep_ld, PREP_LOADS * 16)
            e.wait_ge(os_copied, NB + 1)
            e.transpose(PS[:, 7, 0:2 * KT], gain_rows[:, :], ident[0:2 * KT, 0:2 * KT])
            for i in range(2):
                c = 2 * KT + i * 4 * FT
                e.transpose(PS[:, 7, c:c + 4 * FT], conv_rows[i][:, :], ident[0:4 * FT, 0:4 * FT])
            for i in range(6):
                n = P if i < 5 else P // 2
                c = i * P if i < 4 else PREP7 + (i - 4) * P
                ins = e.transpose(PS[:, 6 if i < 4 else 7, c:c + n], ffn_rows[0:n, i, :], ident[0:n, 0:n])
            ins.then_inc(prep_full, 1)
            def u_rows_transpose(m):
                e.wait_ge(ucol_ready, 2 * m + 2)
                if m:
                    e.wait_ge(ur_copied, m)
                e.transpose(PS[0:NSAMP + BUF, 7, 0:P], u_col[m % 2][:, :], ident[:, :]).then_inc(ur_full, 1)

            def prefix_transpose(m):
                if m:
                    e.wait_ge(pre_copied, m)
                e.transpose(PS[:, 6, 0:NB * BUF], sp_rows[:, m * P:(m + 1) * P],
                            ident[0:NB * BUF, 0:NB * BUF]).then_inc(pre_full, 1)

            for m in range(KT):
                pe_fm_tile(e, N_U + m, m % 2, act_hi, act_lo)
                if m == 0:
                    e.wait_ge(sp_ld, 16)
                    e.wait_ge(prep_done, 1)
                    prefix_transpose(0)
                else:
                    u_rows_transpose(m - 1)
                if m + 1 < KT:
                    prefix_transpose(m + 1)
            pairs(e, N_GP, lambda n, m, slot: pe_fm_tile(e, n, slot, act_hi, act_lo))
            u_rows_transpose(KT - 1)
            pairs(e, N_GA, lambda n, m, slot: pe_fm_tile(e, n, slot, act_hi, act_lo))
            e.wait_ge(ur_copied, KT)
            pe_o_transposes(e, 0, NSAMP)
            for m in range(KT):
                pe_fm_tile(e, N_PL + m, m % 2, act_hi, act_lo, k0=m // 2 * 2, kts=2, ready=d_tail)
            for m in range(2):
                pe_fm_tile(e, N_PB + m, m, act_hi, act_lo, ready=po_tail)
                pe_o_transposes(e, m + 1, P)
            with e.Fori(0, KT // 2 - 1) as i:
                for slot in range(2):
                    pe_fm_tile(e, N_PB + 2 + i * 2 + slot, slot, act_hi, act_lo)
                    pe_o_transposes(e, i * 2 + slot + 3, P)
            for m in range(2):
                pe_fm_tile(e, N_AB + m, m, act_hi, act_lo, ready=o_tail)
            with e.Fori(0, KT // 2 - 1) as i:
                for slot in range(2):
                    pe_fm_tile(e, N_AB + 2 + i * 2 + slot, slot, act_hi, act_lo)

        def act_phase3(e):
            phase2_over(e)
            e.wait_ge(prep_full, 1)
            for m in range(KT):
                n = N_U + m
                fm_head(e, n + 1, 1 - m % 2)
                if m == 0:
                    e.wait_ge(zeros_set, 1)
                    e.wait_ge(prep_done, 1)
                ext = u_ext[m % 2]
                if m >= 2:
                    e.wait_ge(d_done, m - 1)
                    e.wait_ge(ucol_ready, 2 * m - 2)
                samples = ext[:, BUF + SEQ:UE].rearrange("p (b x) -> p b x", b=NB)
                e.wait_ge(pre_full, m + 1)
                e.activation(samples[:, :, 0:BUF], PS[:, 6, 0:NB * BUF].rearrange("p (b x) -> p b x", b=NB),
                             ACT.Copy).then_inc(pre_copied, 1)
                fm_done(e, n)
                b = 3 * (m % 2)
                e.activation(ext[:, BUF:BUF + 2 * CW].rearrange("p (a b) -> p a b", a=2), PS[:, b:b + 2, 0:CW], ACT.Copy)
                e.activation(ext[:, BUF + 2 * CW:BUF + SEQ], PS[:, b + 2, 0:SEQ - 2 * CW], ACT.Copy).then_inc(u_ready, 1)
                e.activation(samples[:, :, BUF:BUF + NS],
                             PS[:, b + 2, SEQ - 2 * CW:TOK - 2 * CW].rearrange("p (b x) -> p b x", b=NB),
                             ACT.Copy).then_inc(fm_free, 1)
                if m:
                    act_u_rows(e, m - 1)

            def gate(dst):
                def body(n, m, slot):
                    fm_head(e, n + 1, 1 - slot)
                    fm_done(e, n)
                    for ps, lo, hi in fm_parts(slot):
                        ins = e.activation(cols(flat(dst, m), lo, hi), ps, ACT.Sigmoid)
                    ins.then_inc(fm_free, 1)
                return body

            pairs(e, N_GP, gate(sig_p))
            act_u_rows(e, KT - 1)
            e.wait_ge(d_done, KT)
            e.wait_ge(ur_st, UR_STORES * 16)
            with e.Fori(0, KT // 2 - 1) as i:
                for slot in range(2):
                    gate(sig_a)(N_GA + i * 2 + slot, i * 2 + slot, slot)
            gate(sig_a)(N_PL - 2, KT - 2, 0)
            fm_head(e, N_PL, 0, 2)
            fm_done(e, N_PL - 1)
            for ps, lo, hi in fm_parts(1):
                ins = e.activation(cols(sig_a[:, KT - 1, :], lo, hi), ps, ACT.Sigmoid)
            ins.then_inc(fm_free, 1)
            for kt in range(4):
                e.activation(act_hi[:, kt, :], dT[:, kt, :], ACT.Copy).then_inc(d_head, 1)
            for g in range(NG):
                n = N_PL + 2 * g
                fm_head(e, n + 1, 1, 2)
                if g < NG - 2:
                    for kt in (2 * g + 4, 2 * g + 5):
                        e.activation(act_hi[:, kt, :], dT[:, kt, :], ACT.Copy).then_inc(d_head, 1)
                for k in range(2):
                    m = 2 * g + k
                    fm_done(e, n + k)
                    for ps, lo, hi in fm_parts(k):
                        ins = e.activation(cols(dT[:, m, :], lo, hi), ps, ACT.Copy,
                                           scale=gain_fm[:, KT + m:KT + m + 1])
                    ins.then_inc(fm_free, 1)
                    if k == 0:
                        fm_head(e, n + 2, 0, 2 if g < NG - 1 else KT)
                for k in range(2):
                    m = 2 * g + k
                    e.wait_ge(fm_free, n + k + 3)
                    e.activation(act_hi[:, m, :], dT[:, m, :], ACT.Copy).then_inc(po_head, 1)
            pairs(e, N_PB, lambda n, m, slot: fm_head(e, n + 1, 1 - slot))
            e.wait_ge(ot_done, 2 * TT)
            fm_done(e, N_AB - 1)
            for kt in range(KT):
                e.activation(act_hi[:, kt, :], oT[:, kt, :], ACT.Copy).then_inc(o_head, 1)

            def merged_head(n, m, slot):
                fm_head(e, n + 1, 1 - slot)
                e.wait_ge(m_sum, m + 1)
                e.activation(flat(m_hi, m), flat(sig_a, m), ACT.Copy).then_inc(m_head, 1)

            with e.Fori(0, KT // 2 - 1) as i:
                for slot in range(2):
                    merged_head(N_AB + i * 2 + slot, i * 2 + slot, slot)
            merged_head(N_UP - 2, KT - 2, 0)
            fm_head(e, N_UP, 0)
            fm_done(e, N_UP - 1)
            for kt in range(2):
                act_wo_head(e, kt)
            e.wait_ge(m_sum, KT)
            e.activation(m_hi[:, KT - 1, :], sig_a[:, KT - 1, :], ACT.Copy).then_inc(m_head, 1)

        def act_u_rows(e, m):
            e.wait_ge(ur_full, m + 1)
            e.activation(u_rows[:, m * P:(m + 1) * P], PS[0:NSAMP + BUF, 7, 0:P], ACT.Copy).then_inc(ur_copied, 1)

        def dve_pool_tile(e, step, m):
            e.wait_ge(u_ready, m + 1)
            e.wait_ge(fm_free, m + 3)
            win = 2 << (m // 2)
            s, sh, k = u_ext[m % 2], 1, 0
            while sh < win:
                dst = u_sum[k % 2]
                a = 2 * sh - 1
                step(e.tensor_tensor(dst[:, a:UE], s[:, a:UE], s[:, a - sh:UE - sh], ALU.add))
                s, sh, k = dst, 2 * sh, k + 1
            ext = u_ext[m % 2]
            e.scalar_tensor_tensor(out=dT[:, m, 0:SEQ], in0=s[:, BUF:BUF + SEQ], scalar=1.0 / win,
                                   in1=ext[:, BUF:BUF + SEQ], op0=ALU.mult, op1=ALU.subtract)
            v = s[:, BUF + SEQ:UE].rearrange("p (b x) -> p b x", b=NB)
            x = ext[:, BUF + SEQ:UE].rearrange("p (b x) -> p b x", b=NB)
            step(e.scalar_tensor_tensor(out=dT[:, m, SEQ:TOK].rearrange("p (b x) -> p b x", b=NB),
                                        in0=v[:, :, BUF:BUF + NS], scalar=1.0 / win, in1=x[:, :, BUF:BUF + NS],
                                        op0=ALU.mult, op1=ALU.subtract))
            w = win - 1
            step(e.tensor_tensor(dT[:, m, 0:w], s[:, BUF:BUF + w], inv_cnt[:, 0:w], ALU.mult))
            e.tensor_tensor(dT[:, m, 0:w], dT[:, m, 0:w], ext[:, BUF:BUF + w], ALU.subtract).then_inc(d_done, 1)

        def dve_normalize_o(e, step, idx, n_rows=P):
            e.wait_ge(o_ld, idx * 16 + 16)
            o, s = o_tile[0:n_rows, :], sst[0:n_rows, 0, 0:NH]
            step(e.tensor_tensor(o_sq[0:n_rows, :], o, o, ALU.mult))
            e.tensor_reduce(s, o_sq[0:n_rows, :].rearrange("p (h d) -> p h d", h=NH), AX.X,
                            ALU.add).then_inc(sumsq_o, 1)
            e.wait_ge(rstd_o, idx + 1)
            v = o.rearrange("p (h d) -> p h d", h=NH)
            e.tensor_tensor(v, v, rst[0:n_rows, 0, 0:NH].unsqueeze(2).to_broadcast([n_rows, NH, VD]), ALU.mult).then_inc(scaled_o, 1)

        def dve_take_o(e, idx, n_rows, c0):
            e.wait_ge(o_tr, idx * 2 + 2)
            for half in range(2):
                ps = PS[:, 6 + half, :].rearrange("p (a b) -> p a b", a=4)[:, :, 0:n_rows]
                g = gain_fm[:, 4 * half:4 * half + 4].unsqueeze(2).to_broadcast([P, 4, n_rows])
                e.tensor_tensor(oT[:, 4 * half:4 * half + 4, bass.ds(c0, n_rows)], ps, g, ALU.mult).then_inc(ot_done, 1)

        def dve_phase3(e, step):
            e.wait_ge(prep_full, 1)
            e.tensor_scalar(gain_fm[:, 0:KT], PS[:, 7, 0:KT], 1.0 - LAMBDA_INIT, None, ALU.mult)
            e.tensor_copy(gain_fm[:, KT:2 * KT], PS[:, 7, KT:2 * KT])
            e.tensor_copy(conv_c[:, :, :].rearrange("p a b -> p (a b)"), PS[:, 7, 2 * KT:PREP7])
            pre = ffn_pre[:, :, :, :].rearrange("p a b c -> p (a b c)")
            e.tensor_copy(pre[:, 0:4 * P], PS[:, 6, :])
            e.tensor_copy(pre[:, 4 * P:4 * P + 3 * P // 2], PS[:, 7, PREP7:PREP7 + 3 * P // 2]).then_inc(prep_done, 1)
            for m in range(KT):
                dve_pool_tile(e, step, m)
            dve_normalize_o(e, step, 0, NSAMP)
            for kt in range(4):
                dve_d_tail(e, kt)
            for g in range(NG):
                if g < NG - 2:
                    dve_d_tail(e, 2 * g + 4)
                    dve_d_tail(e, 2 * g + 5)
                for k in range(2):
                    m = 2 * g + k
                    e.wait_ge(po_head, m + 1)
                    e.tensor_tensor(act_lo[:, m, :], dT[:, m, :], act_hi[:, m, :].bitcast(F32),
                                    ALU.subtract).then_inc(po_tail, 1)
            e.wait_ge(po_tail, KT)
            dve_take_o(e, 0, NSAMP, SEQ)
            n0 = step.n
            with e.Fori(0, KT // 2) as i:
                step.n = n0 + i * 2
                for slot in range(2):
                    m = i * 2 + slot
                    dve_normalize_o(e, step, m + 1)
                    fm_done(e, N_PB + m)
                    for ps, lo, hi in fm_parts(slot):
                        v = cols(flat(sig_p, m), lo, hi)
                        ins = e.tensor_tensor(v, ps, v, ALU.mult)
                    ins.then_inc(fm_free, 1)
                    dve_take_o(e, m + 1, P, m * P)
            step.n = n0 + KT
            for kt in range(KT):
                e.wait_ge(o_head, kt + 1)
                e.tensor_tensor(act_lo[:, kt, :], oT[:, kt, :], act_hi[:, kt, :].bitcast(F32),
                                ALU.subtract).then_inc(o_tail, 1)

            def merge(m, slot, between=lambda kt: None):
                fm_done(e, N_AB + m)
                for ps, lo, hi in fm_parts(slot):
                    v = cols(flat(sig_a, m), lo, hi)
                    ins = e.tensor_tensor(v, ps, v, ALU.mult)
                ins.then_inc(fm_free, 1)
                between(0)
                e.wait_ge(fm_free, N_AB + m + 3)
                e.tensor_tensor(flat(sig_a, m), flat(sig_a, m), flat(sig_p, m), ALU.add).then_inc(m_sum, 1)
                between(1)
                e.wait_ge(m_head, m + 1)
                e.tensor_tensor(flat(m_lo, m), flat(sig_a, m), flat(m_hi, m).bitcast(F32),
                                ALU.subtract).then_inc(m_tail, 1)

            with e.Fori(0, KT // 2 - 1) as i:
                for slot in range(2):
                    merge(i * 2 + slot, slot)
            merge(KT - 2, 0)
            merge(KT - 1, 1, lambda kt: dve_wo_tail(e, kt))

        def dve_d_tail(e, kt):
            e.wait_ge(d_head, kt + 1)
            e.tensor_tensor(act_lo[:, kt, :], dT[:, kt, :], act_hi[:, kt, :].bitcast(F32),
                            ALU.subtract).then_inc(d_tail, 1)

        def pool_phase3(e, step):
            for i in range(16):
                step(e.memset(inv_cnt[:, i:i + 1], 1.0 / (i + 1)))
            phase2_over(e)
            step(e.memset(u_ext[0][:, 0:BUF], 0.0))
            e.memset(u_ext[1][:, 0:BUF], 0.0).then_inc(zeros_set, 1)
            for m in range(KT):
                fm_tail(e, m + 1, 1 - m % 2)
                e.wait_ge(u_ready, m + 1)
                e.wait_ge(fm_free, m + 3)
                if m >= 2:
                    e.wait_ge(ur_full, m - 1)
                x = u_ext[m % 2]
                e.tensor_copy(u_col[m % 2][:, 0:NSAMP].rearrange("p (b q) -> p b q", b=NB),
                              x[:, BUF + SEQ:UE].rearrange("p (b x) -> p b x", b=NB)[:, :, BUF:BUF + NS]
                              ).then_inc(ucol_ready, 1)
                e.tensor_copy(u_col[m % 2][:, NSAMP:NSAMP + BUF], x[:, SEQ:SEQ + BUF]).then_inc(ucol_ready, 1)
            pairs(e, N_GP, lambda n, m, slot: fm_tail(e, n + 1, 1 - slot))
            with e.Fori(0, KT // 2 - 1) as i:
                for slot in range(2):
                    fm_tail(e, N_GA + i * 2 + slot + 1, 1 - slot)
            pool_rstd_o(e, step, 0)
            fm_tail(e, N_PL - 1, 1)
            for m in range(KT):
                fm_tail(e, N_PL + m, m % 2, 2)
            fm_tail(e, N_PB, 0)
            n0 = step.n
            with e.Fori(0, KT // 2) as i:
                step.n = n0 + i * 4
                for slot in range(2):
                    m = i * 2 + slot
                    pool_rstd_o(e, step, m + 1)
                    fm_tail(e, N_PB + m + 1, 1 - slot)
            step.n = n0 + 2 * KT
            pairs(e, N_AB, lambda n, m, slot: fm_tail(e, n + 1, 1 - slot))

        def pool_rstd_o(e, step, idx):
            e.wait_ge(sumsq_o, idx + 1)
            pool_rstd(e, step, rst[:, 0, 0:NH], sst[:, 0, 0:NH], NH, VD).then_inc(rstd_o, 1)

        PREP7 = 2 * KT + 8 * FT
        PREP_LOADS = 2 + 4 + 2 * FT
        UR_STORES = 1 + NB + 1

        def w_in_cols(c):
            return w_in_v[:, :, bass.ds(c, P)]

        def matrix_cols(w):
            v = w[0].rearrange("(kt p) n -> p kt n", p=P)
            return lambda c: v[:, :, bass.ds(c, P)]

        def sp_prefetch_phase3(e):
            fm_load(e, 0, w_in_cols(COL_U))
            e.dma_start(gain_rows[0:KT, :], head_norm[0]).then_inc(prep_ld, 16)
            e.dma_start(gain_rows[KT:2 * KT, :], pool_scale[0].rearrange("g (a p) -> (g a) p", p=P)).then_inc(prep_ld, 16)
            for j in range(4):
                src = conv_w[0, j, :] if j < 3 else conv_b[0, :]
                e.dma_start(conv_rows[j // 2][j % 2 * 2 * FT:(j % 2 + 1) * 2 * FT, :],
                            src.rearrange("(a p) -> a p", p=P)).then_inc(prep_ld, 16)
            for a in range(2 * FT):
                e.dma_start(ffn_rows[a % 8 * NB * 2:(a % 8 + 1) * NB * 2, a // 8, :],
                            state_ffn_conv[0].rearrange("b r n -> (b r) n")[:, a * P:(a + 1) * P]).then_inc(prep_ld, 16)

        def sp_phase3(e):
            phase2_over(e)
            e.dma_start(sp_rows[:, :], state_pool[0].rearrange("b r n -> (b r) n")).then_inc(sp_ld, 16)
            e.dma_start(o_tile[0:NSAMP, :], o_dram[SEQ:TOK, :]).then_inc(o_ld, 16)
            e.dma_start(pool_sample[0, :, 0:BUF - NS, :], state_pool[0, :, NS:BUF, :]).then_inc(ur_st, 16)
            for m in range(1, KT):
                fm_load(e, N_U + m, w_in_cols(COL_U + m * P))
            with e.Fori(0, KT) as i:
                fm_load(e, N_GP + i, w_in_cols(COL_GP + i * P))
            fm_load(e, N_GA, w_in_cols(COL_GA))
            e.wait_ge(ur_copied, KT)
            e.dma_start(pool_prompt[0, 0], u_rows[NSAMP:NSAMP + BUF, :]).then_inc(ur_st, 16)
            for b in range(NB):
                e.dma_start(pool_sample[0, b, BUF - NS:BUF, :], u_rows[b * NS:(b + 1) * NS, :]).then_inc(ur_st, 16)
            with e.Fori(0, KT - 1) as i:
                fm_load(e, N_GA + 1 + i, w_in_cols(COL_GA + P + i * P))
            for m in range(KT):
                fm_load(e, N_PL + m, w_pool[0, m // 2].rearrange("(kt p) n -> p kt n", p=P)[:, :, m % 2 * P:(m % 2 + 1) * P])
            fm_load(e, N_PB, matrix_cols(w_pool_branch)(0))
            with e.Fori(0, KT - 1) as i:
                e.wait_ge(o_tr, i * 2 + 2)
                e.dma_start(o_tile[:, :], o_dram[bass.ds(i * P, P), :]).then_inc(o_ld, 16)
                fm_load(e, N_PB + 1 + i, matrix_cols(w_pool_branch)(P + i * P))
            e.wait_ge(o_tr, 2 * TT - 2)
            e.dma_start(o_tile[:, :], o_dram[SEQ - P:SEQ, :]).then_inc(o_ld, 16)
            fm_load(e, N_AB, matrix_cols(w_attn_branch)(0))
            with e.Fori(0, KT - 1) as i:
                fm_load(e, N_AB + 1 + i, matrix_cols(w_attn_branch)(P + i * P))
                e.wait_ge(m_sum, i + 1)
                e.dma_start(wo_raw[:, bass.ds(i, 1), :], w_out[0, bass.ds(i * P, P), :].unsqueeze(1)).then_inc(wo_ld, 16)
            fm_load(e, N_UP, matrix_cols(w_up)(0))
            e.wait_ge(m_sum, KT)
            e.dma_start(wo_raw[:, KT - 1, :], w_out[0, D - P:D, :]).then_inc(wo_last, 16)

        wo_raw = at("wo_raw", [P, KT, D], F32, R3)
        x1 = at("x1", [P, TT, D], F32, R3)
        wo_hi = at("wo_hi", [P, KT, D], F32R, R1)
        wo_lo = at("wo_lo", [P, KT, D], F32R, R1 + fit(KT, D))
        gain_h = at("gain_h", [P, D], F32, R1 + 2 * fit(KT, D))
        xn = at("xn", [P, D], F32, R3 + fit(TT, D))
        wo_ld = sem("wo_ld")
        wo_last = sem("wo_last")
        wo_head = sem("wo_head")
        wo_tail = sem("wo_tail")
        wo_full = sem("wo_full")
        x1_ld = sem("x1_ld")
        x1_done = sem("x1_done")
        gain_h_ld = sem("gain_h_ld")
        sumsq_h = sem("sumsq_h")
        rstd_h = sem("rstd_h")
        xn_h = sem("xn_h")
        tr_h = sem("tr_h")
        hi_h = sem("hi_h")
        lo_h = sem("lo_h")

        def pe_phase4(e):
            for t in range(TT):
                if t < 2:
                    e.wait_ge(fm_free, N_UP + 1 + t)
                if t >= 2:
                    e.wait_ge(x1_done, t - 1)
                for kt in range(KT):
                    if t == 0:
                        e.wait_ge(wo_tail, kt + 1)
                        e.wait_ge(m_tail, kt + 1)
                    m_h = m_hi[:, kt, t * P:t * P + rows(t)]
                    m_l = m_lo[:, kt, t * P:t * P + rows(t)]
                    for a, w, first, last in ((m_h, wo_hi, True, False), (m_h, wo_lo, False, False), (m_l, wo_hi, False, True)):
                        for half in range(2):
                            ins = e.matmul(PS[0:rows(t), 2 * (t % 2) + half, :], a, w[:, kt, half * 512:(half + 1) * 512],
                                           start=first and kt == 0, stop=last and kt == KT - 1)
                ins.then_inc(wo_full, 1)
                if t:
                    pe_h_transposes(e, t - 1)
        def pe_h_transposes(e, t):
            e.wait_ge(xn_h, t + 1)
            for half in range(2):
                if t:
                    e.wait_ge(lo_h, 2 * (t - 1) + half + 1)
                for j in range(4):
                    kt = 4 * half + j
                    ins = e.transpose(PS[:, 6 + half, j * P:j * P + rows(t)], xn[0:rows(t), kt * P:(kt + 1) * P],
                                      ident[0:rows(t), 0:rows(t)])
                ins.then_inc(tr_h, 1)

        def h_half(t, half):
            ps = PS[:, 6 + half, :].rearrange("p (a b) -> p a b", b=P)[:, :, 0:rows(t)]
            s = (slice(None), slice(4 * half, 4 * half + 4), slice(t * P, t * P + rows(t)))
            return ps, m_hi[s], m_lo[s]

        def act_wo_head(e, kt):
            e.wait_ge(wo_ld, 16 * (KT - 1))
            if kt == KT - 1:
                e.wait_ge(wo_last, 16)
            e.activation(wo_hi[:, kt, :], wo_raw[:, kt, :], ACT.Copy).then_inc(wo_head, 1)

        def dve_wo_tail(e, kt):
            e.wait_ge(wo_head, kt + 1)
            e.tensor_tensor(wo_lo[:, kt, :], wo_raw[:, kt, :], wo_hi[:, kt, :].bitcast(F32),
                            ALU.subtract).then_inc(wo_tail, 1)

        def act_phase4(e):
            for kt in range(2, KT):
                act_wo_head(e, kt)
            for t in range(TT + 1):
                if t < TT:
                    e.wait_ge(x1_done, t + 1)
                    if t:
                        e.wait_ge(sumsq_h, t)
                    e.activation(PS[0:rows(t), 4:6, :].rearrange("p a b -> p (a b)"), x1[0:rows(t), t, :], ACT.Square,
                                 accum_out=sst[0:rows(t), t % 4, 0:1]).then_inc(sumsq_h, 1)
                if t:
                    for half in range(2):
                        e.wait_ge(tr_h, 2 * (t - 1) + half + 1)
                        ps, hi, _ = h_half(t - 1, half)
                        e.activation(hi, ps, ACT.Copy).then_inc(hi_h, 1)

        def dve_phase4(e, step):
            for kt in range(2, KT):
                dve_wo_tail(e, kt)
            e.wait_ge(x1_ld, 16 * TT)
            e.wait_ge(gain_h_ld, 16)
            for t in range(TT):
                e.wait_ge(wo_full, t + 1)
                v = x1[0:rows(t), t, :].rearrange("p (a b) -> p a b", a=2)
                e.tensor_tensor(v, v, PS[0:rows(t), 2 * (t % 2):2 * (t % 2) + 2, :], ALU.add).then_inc(x1_done, 1)
                if t:
                    dve_h_tail(e, t - 1)
                e.wait_ge(rstd_h, t + 1)
                e.scalar_tensor_tensor(out=xn[0:rows(t), :], in0=x1[0:rows(t), t, :], scalar=rst[0:rows(t), t % 4, 0:1],
                                       in1=gain_h[0:rows(t), :], op0=ALU.mult, op1=ALU.mult).then_inc(xn_h, 1)
            dve_h_tail(e, TT - 1)

        def dve_h_tail(e, t):
            for half in range(2):
                e.wait_ge(hi_h, 2 * t + half + 1)
                ps, hi, lo = h_half(t, half)
                e.tensor_tensor(lo, ps, hi.bitcast(F32), ALU.subtract).then_inc(lo_h, 1)

        def pool_phase4(e, step):
            for t in range(TT):
                e.wait_ge(sumsq_h, t + 1)
                pool_rstd(e, step, rst[:, t % 4, 0:1], sst[:, t % 4, 0:1], 1, D).then_inc(rstd_h, 1)

        def sp_phase4(e):
            for t in range(TT):
                e.wait_ge(wo_tail, min(t, KT - 1) + 1)
                src = x_prompt[0, t * P:(t + 1) * P, :] if t < QT else x_sample.rearrange("b q d -> (b q) d")
                e.dma_start(x1[0:rows(t), t, :], src).then_inc(x1_ld, 16)
                if t == 0:
                    e.dma_start(gain_h[:, :], norm_ffn[0:1, :].to_broadcast([P, D])).then_inc(gain_h_ld, 16)

        UNITS = FT // 2
        FE = 2 + SEQ + NB * (2 + NS)
        FC = FE - 2
        r = Region(R1, X0)
        f_hi = [r(f"f_hi{i}", [P, TOK], F32R) for i in range(4)]
        f_lo = [r(f"f_lo{i}", [P, TOK], F32R) for i in range(4)]
        f_ext = [r(f"f_ext{i}", [P, FE]) for i in range(2)]
        f_c = [r(f"f_c{i}", [P, FE]) for i in range(2)]
        wd_hi = [r(f"wd_hi{i}", [P, D], F32R) for i in range(2)]
        wd_lo = [r(f"wd_lo{i}", [P, D], F32R) for i in range(2)]
        r = Region(R3 + fit(TT, D), STREAM)
        wd_raw = r("wd_raw", [P, D])
        st_rows = r("st_rows", [2 + 2 * NB, 4 * P])
        DOWN_USES = 2 * TT + 2

        f_zeros = sem("f_zeros")
        ext_ready = sem("ext_ready")
        conv_done = sem("conv_done")
        st_copied = sem("st_copied")
        silu_done = sem("silu_done")
        prod_ready = sem("prod_ready")
        f_head = sem("f_head")
        f_tail = sem("f_tail")
        wd_ld = sem("wd_ld")
        wd_head = sem("wd_head")
        wd_tail = sem("wd_tail")
        dn_full = sem("dn_full")
        dn_free = sem("dn_free")
        st_st = sem("st_st")
        y_st = sem("y_st")

        def each_unit(e, body, last):
            body(0, 0, False)
            with e.Fori(0, (UNITS - 3) // 2) as i:
                body(i * 2 + 1, 1, False)
                body(i * 2 + 2, 0, False)
            body(UNITS - 2, 1, False)
            body(UNITS - 1, 0, True)
            last(UNITS, 1)

        def samples(tile, rows_):
            return tile[:, 2 + SEQ:FE].rearrange("p (b x) -> p b x", b=NB)[:, :, rows_]

        def pe_down(e, j, par):
            e.wait_ge(st_copied, 4 * j + 4)
            for u in range(DOWN_USES):
                use = j * DOWN_USES + u
                e.wait_ge(dn_free, use + 1)
                bank = 6 + u % 2
                if u < 2:
                    for k in range(2):
                        ins = e.transpose(PS[0:2 + 2 * NB, bank, k * P:(k + 1) * P], st_col[par][:, 2 * u + k, :], ident[:, :])
                else:
                    if u == 2:
                        e.wait_ge(f_tail, 2 * j + 2)
                        e.wait_ge(wd_tail, 2 * j + 2)
                    t, half = divmod(u - 2, 2)
                    for k in range(2):
                        f_h = f_hi[2 * par + k][:, t * P:t * P + rows(t)]
                        f_l = f_lo[2 * par + k][:, t * P:t * P + rows(t)]
                        for a, w, first, last in ((f_h, wd_hi, True, False), (f_h, wd_lo, False, False), (f_l, wd_hi, False, True)):
                            ins = e.matmul(PS[0:rows(t), bank, :], a, w[k][:, half * 512:(half + 1) * 512],
                                           start=first and k == 0, stop=last and k == 1)
                ins.then_inc(dn_full, 1)

        def pe_phase5(e):
            def before_chunk(c):
                if c == 0:
                    e.wait_ge(lo_h, 2 * 6)
                    e.wait_ge(x1_done, TT)
                elif c == 1:
                    pe_h_transposes(e, TT - 1)
                else:
                    e.wait_ge(lo_h, 2 * TT)

            def unit(j, par, end):
                for q in range(4):
                    if q == 0 and not after_first(j):
                        pe_fm_tile_by_chunk(e, N_UP, 0, m_hi, m_lo, before_chunk)
                    else:
                        pe_fm_tile(e, N_UP + 4 * j + q, q % 2, m_hi, m_lo)
                    if q == 0 and after_first(j):
                        pe_down(e, j - 1, 1 - par)

            each_unit(e, unit, lambda j, par: pe_down(e, j - 1, 1 - par))

        def act_f_head(e, j, par, k):
            e.wait_ge(prod_ready, 2 * j + k + 1)
            i = 2 * par + k
            e.activation(f_hi[i][:, 0:SEQ], f_c[1][:, 0:SEQ], ACT.Copy)
            e.activation(f_hi[i][:, SEQ:TOK].rearrange("p (b x) -> p b x", b=NB), samples(f_c[1], slice(0, NS)),
                         ACT.Copy).then_inc(f_head, 1)

        def act_phase5(e):
            e.wait_ge(f_zeros, 1)
            def unit(j, par, end):
                for q in range(4):
                    x = 4 * j + q
                    n = N_UP + x
                    if q < 3 or not end:
                        fm_head(e, n + 1, (q + 1) % 2)
                    if q == 0 and after_first(j):
                        act_f_head(e, j - 1, 1 - par, 1)
                    if q == 2:
                        act_f_head(e, j, par, 0)
                    if q % 2:
                        e.wait_ge(conv_done, x)
                        e.activation(f_c[0][:, 0:FC], f_c[0][:, 0:FC], ACT.Silu).then_inc(silu_done, 1)
                    if q >= 2:
                        k = q - 2
                        e.wait_ge(wd_ld, (2 * j + k) * 16 + 16)
                        e.wait_ge(dn_full, j * DOWN_USES)
                        e.activation(wd_hi[k][:, :], wd_raw[:, :], ACT.Copy).then_inc(wd_head, 1)
                    if after_first(j) or q >= 2:
                        e.wait_ge(conv_done, x - 1)
                    fm_done(e, n)
                    ext, b = f_ext[q % 2], 3 * (q % 2)
                    e.activation(ext[:, 2:2 + 2 * CW].rearrange("p (a b) -> p a b", a=2), PS[:, b:b + 2, 0:CW], ACT.Copy)
                    e.activation(ext[:, 2 + 2 * CW:2 + SEQ], PS[:, b + 2, 0:SEQ - 2 * CW], ACT.Copy)
                    e.activation(samples(ext, slice(2, 2 + NS)),
                                 PS[:, b + 2, SEQ - 2 * CW:TOK - 2 * CW].rearrange("p (b x) -> p b x", b=NB),
                                 ACT.Copy).then_inc(fm_free, 1)
                    a = (q % 2) * FT + 2 * j + q // 2
                    pre = ffn_pre[:, :, :, :].rearrange("p a b c -> p (a b) c")[:, bass.ds(a, 1), :]
                    e.activation(samples(ext, slice(0, 2)), pre.rearrange("p a (b r) -> p (a b) r", b=NB),
                                 ACT.Copy).then_inc(ext_ready, 1)

            each_unit(e, unit, lambda j, par: act_f_head(e, j - 1, 1 - par, 1))

        def dve_conv(e, step, j, par, q):
            x = 4 * j + q
            e.wait_ge(ext_ready, x + 1)
            dst = st_col[par][:, 2 * (q % 2) + q // 2, :]
            e.tensor_copy(dst[:, 0:2], f_ext[q % 2][:, SEQ:SEQ + 2])
            e.tensor_copy(dst[:, 2:2 + 2 * NB].rearrange("p (b r) -> p b r", b=NB),
                          samples(f_ext[q % 2], slice(NS, NS + 2))).then_inc(st_copied, 1)
            a = (q % 2) * FT + 2 * j + q // 2
            tap = [conv_c[:, i, bass.ds(a, 1)] for i in range(4)]
            ext, c = f_ext[q % 2], f_c[q % 2][:, 0:FC]
            step(e.tensor_scalar(c, ext[:, 2:FE], tap[2], tap[3], ALU.mult, ALU.add))
            step(e.scalar_tensor_tensor(out=c, in0=ext[:, 1:FE - 1], scalar=tap[1], in1=c, op0=ALU.mult, op1=ALU.add))
            e.scalar_tensor_tensor(out=c, in0=ext[:, 0:FC], scalar=tap[0], in1=c, op0=ALU.mult, op1=ALU.add
                                   ).then_inc(conv_done, 1)

        def dve_product(e, j, par, k):
            e.wait_ge(silu_done, 2 * j + k + 1)
            e.wait_ge(conv_done, 4 * j + 2 * k + 2)
            e.tensor_tensor(f_c[1][:, 0:FC], f_c[1][:, 0:FC], f_c[0][:, 0:FC], ALU.mult).then_inc(prod_ready, 1)
            e.wait_ge(f_head, 2 * j + k + 1)
            i = 2 * par + k
            e.tensor_tensor(f_lo[i][:, 0:SEQ], f_c[1][:, 0:SEQ], f_hi[i][:, 0:SEQ].bitcast(F32), ALU.subtract)
            e.tensor_tensor(f_lo[i][:, SEQ:TOK].rearrange("p (b x) -> p b x", b=NB), samples(f_c[1], slice(0, NS)),
                            f_hi[i][:, SEQ:TOK].bitcast(F32).rearrange("p (b x) -> p b x", b=NB),
                            ALU.subtract).then_inc(f_tail, 1)

        def dve_down(e, j):
            for u in range(DOWN_USES):
                e.wait_ge(dn_full, j * DOWN_USES + u + 1)
                bank = 6 + u % 2
                if u < 2:
                    if u == 0 and after_first(j):
                        e.wait_ge(st_st, 32 * j + 1)
                    ins = e.tensor_copy(st_rows[:, u * 2 * P:(u + 1) * 2 * P], PS[0:2 + 2 * NB, bank, 0:2 * P])
                else:
                    t, half = divmod(u - 2, 2)
                    v = x1[0:rows(t), t, half * 512:(half + 1) * 512]
                    ins = e.tensor_tensor(v, v, PS[0:rows(t), bank, :], ALU.add)
                ins.then_inc(dn_free, 1)

        def dve_phase5(e, step):
            e.sem_inc(dn_free, 2)
            n0 = step.n

            def unit(j, par, end):
                step.n = n0 + j * 8
                if after_first(j):
                    dve_down(e, j - 1)
                for q in range(4):
                    dve_conv(e, step, j, par, q)
                    if q % 2:
                        dve_product(e, j, par, q // 2)

            each_unit(e, unit, lambda j, par: dve_down(e, j - 1))

        def pool_phase5(e, step):
            e.wait_ge(wo_full, TT)
            step(e.memset(f_ext[0][:, 0:2], 0.0))
            e.memset(f_ext[1][:, 0:2], 0.0).then_inc(f_zeros, 1)

            def unit(j, par, end):
                for q in range(4):
                    x = 4 * j + q
                    if q < 3 or not end:
                        fm_tail(e, N_UP + x + 1, (q + 1) % 2)
                    if q >= 2:
                        e.wait_ge(wd_head, 2 * j + q - 1)
                        e.tensor_tensor(wd_lo[q - 2][:, :], wd_raw[:, :], wd_hi[q - 2][:, :].bitcast(F32),
                                        ALU.subtract).then_inc(wd_tail, 1)

            each_unit(e, unit, lambda j, par: None)

        w_up_cols = matrix_cols(w_up)

        def sp_wait_states(e, j):
            e.wait_ge(dn_free, j * DOWN_USES + 4)

        def sp_store_states(e, j):
            src = st_rows[:, :].rearrange("p (v x) -> p v x", v=2)
            e.dma_start(ffn_prompt[0, 0].rearrange("r (v x) -> r v x", v=2)[:, :, bass.ds(j * 2 * P, 2 * P)],
                        src[0:2, :, :]).then_inc(st_st, 16)
            e.dma_start(ffn_sample[0].rearrange("b r (v x) -> (b r) v x", v=2)[:, :, bass.ds(j * 2 * P, 2 * P)],
                        src[2:2 + 2 * NB, :, :]).then_inc(st_st, 16)

        def sp_load_down(e, kt):
            if after_first(kt):
                e.wait_ge(wd_tail, kt)
            e.dma_start(wd_raw[:, :], w_down[0, bass.ds(kt * P, P), :]).then_inc(wd_ld, 16)

        def sp_phase5(e):
            def unit(j, par, end):
                for q in range(4):
                    k = q + 1
                    c = 2 * j * P + (k // 2) * P + (FT * P if k % 2 else 0)
                    if q < 3 or not end:
                        fm_load(e, N_UP + 4 * j + k, w_up_cols(c),
                                (lambda: sp_wait_states(e, j - 1)) if q == 2 and after_first(j) else None)
                    if q == 1 and not after_first(j):
                        e.wait_ge(tr_h, 2 * TT)
                    if q == 2 and after_first(j):
                        sp_store_states(e, j - 1)
                    if q >= 1 and q < 3:
                        sp_load_down(e, 2 * j + q - 1)

            each_unit(e, unit, lambda j, par: (sp_wait_states(e, j - 1), sp_store_states(e, j - 1)))
            for t in range(TT):
                e.wait_ge(dn_free, (UNITS - 1) * DOWN_USES + 2 + 4 + 2 * t)
                dst = y_prompt[0, t * P:(t + 1) * P, :] if t < QT else y_sample.rearrange("b q d -> (b q) d")
                e.dma_start(dst, x1[0:rows(t), t, :]).then_inc(y_st, 16)
            e.wait_ge(y_st, 16 * TT)
            e.wait_ge(st_st, 32 * UNITS + 1)

        block = ctx.enter_context(nc.Block())

        @block.sync
        def _(e):
            sp_phase1(e)
            sp_phase2(e)
            sp_phase3(e)
            sp_phase4(e)
            sp_phase5(e)

        @block.gpsimd
        def _(e):
            step = Step(e, pool_step)
            pool_constants(e, step)
            pool_phase1(e, step)
            pool_phase2(e, step)
            pool_phase3(e, step)
            pool_phase4(e, step)
            pool_phase5(e, step)

        @block.scalar
        def _(e):
            act_phase1(e)
            act_phase2(e)
            act_phase3(e)
            act_phase4(e)
            act_phase5(e)

        @block.vector
        def _(e):
            step = Step(e, dve_step)
            dve_phase1(e, step)
            dve_phase2(e, step)
            dve_phase3(e, step)
            dve_phase4(e, step)
            dve_phase5(e, step)

        @block.tensor
        def _(e):
            pe_phase1(e)
            pe_phase2(e)
            pe_phase3(e)
            pe_phase4(e)
            pe_phase5(e)


_INS = ['x_prompt', 'x_sample', 'cache_k', 'cache_v', 'state_pool', 'state_ffn_conv', 'page_table',
        'norm_mix', 'w_in', 'q_norm', 'k_norm', 'lambda_q1', 'lambda_k1', 'lambda_q2', 'lambda_k2',
        'head_norm', 'w_pool', 'pool_scale', 'w_attn_branch', 'w_pool_branch', 'w_out', 'norm_ffn',
        'w_up', 'conv_w', 'conv_b', 'w_down']


def kernel(**inputs):
    import numpy as _np
    import concourse.bacc as _bacc
    from concourse import mybir as _mybir
    from concourse.bass_utils import run_bass_kernel_spmd as _run

    shape = {n: inputs[n].shape for n in _INS}
    _, seq, d = shape['x_prompt']
    nb, ns, _ = shape['x_sample']
    heads, vd = shape['cache_k'][3:]
    buf, pool_w = shape['state_pool'][2:]
    conv_rows, ff2 = shape['state_ffn_conv'][2:]
    outs = [(1, seq, d), (nb, ns, d), (1, 1, seq, heads, vd), (1, 1, seq, heads, vd),
            (1, 1, buf, pool_w), (1, 1, conv_rows, ff2), (1, nb, ns, heads, vd), (1, nb, ns, heads, vd),
            (1, nb, buf, pool_w), (1, nb, conv_rows, ff2)]
    nc = _bacc.Bacc("TRN2", target_bir_lowering=False, num_devices=1)
    arrays, args = {}, []
    for name in _INS:
        a = _np.ascontiguousarray(inputs[name])
        arrays[f"in_{name}_dram"] = a
        args.append(nc.dram_tensor(f"in_{name}_dram", a.shape, _mybir.dt.from_np(a.dtype), kind="ExternalInput").ap())
    for i, s in enumerate(outs):
        args.append(nc.dram_tensor(f"out_{i}_dram", s, _mybir.dt.float32, kind="ExternalOutput").ap())
    build_step(nc, *args)
    r = _run(nc, [arrays], core_ids=[0])
    return tuple(r.results[0][f"out_{i}_dram"] for i in range(len(outs)))
```
